# Optimizing a Trainium2 kernel written in Bass

```python
import jax, jax.numpy as jnp
from jax import lax
import numpy as np

D_MODEL = 1024
BATCH = 1
SEQ = 256
DEPTH = 1
DEC_BATCH = 8
DEC_SEQ = 8
PAST_LEN = 2048
PAGE_SIZE = 128

D_MIX = D_MODEL
H_A = 4
DK_A = D_MIX // 2 // H_A
DV_A = D_MIX // 2 // H_A
H_B = 4
DV_B = D_MIX // 2 // H_B
DK_B = DV_B // 2
CONV_W = 4
CONV_CH = H_A * (2 * DK_A + DV_A)
CHUNK = 64
N_EXPERTS = 32
TOP_K = 4
D_FF = D_MODEL
SWIGLU_LIMIT = 7.0
SWIGLU_ALPHA = 1.702
MOE_BLOCK = 128
PLE_DIM = 256
EPS = 1e-6
NEG = -1e30
SPLITS = (CONV_CH, H_A * DV_A, H_A, H_A,
          H_B * DK_B, H_B * DK_B, H_B * DV_B, H_B * DV_B, H_B, H_B)
IN_W = sum(SPLITS)

kernel_name = "hymba_gdn_mlstm_moe_ple_step"

def _split(a, sizes):
    return jnp.split(a, [int(s) for s in np.cumsum(sizes)[:-1]], axis=-1)

def _rms(x, g):
    x32 = x.astype(jnp.float32)
    return x32 * lax.rsqrt(jnp.mean(x32 * x32, axis=-1, keepdims=True) + EPS) * g.astype(jnp.float32)

def _l2norm(x):
    return x * lax.rsqrt(jnp.sum(x * x, axis=-1, keepdims=True) + EPS)

def _heads(a, h):
    b, t, _ = a.shape
    return a.reshape(b, t, h, -1).transpose(0, 2, 1, 3)

def _merge(a):
    b, h, t, d = a.shape
    return a.transpose(0, 2, 1, 3).reshape(b, t, h * d)

def _pad_chunks(a, n_c, L, value):
    pad = n_c * L - a.shape[2]
    a = jnp.pad(a, [(0, 0), (0, 0), (0, pad)] + [(0, 0)] * (a.ndim - 3), constant_values=value)
    return a.reshape(a.shape[0], a.shape[1], n_c, L, *a.shape[3:])

def _gated_delta_rule(q, k, v, g, beta, S0):
    B, H, T, _ = q.shape
    L = min(T, CHUNK)
    n_c = -(-T // L)
    q, k, v, g, beta = (_pad_chunks(a, n_c, L, 0.0) for a in (q, k, v, g, beta))
    tril = jnp.tril(jnp.ones((L, L), bool))
    strict = jnp.tril(jnp.ones((L, L), bool), -1)
    gc = jnp.cumsum(g, axis=-1)
    diff = gc[..., :, None] - gc[..., None, :]
    decay = jnp.where(tril, jnp.exp(jnp.where(tril, diff, 0.0)), 0.0)
    kb = k * beta[..., None]
    a_mat = jnp.where(strict, jnp.einsum('bhcid,bhcjd->bhcij', kb, k) * decay, 0.0)
    lhs = a_mat + jnp.eye(L, dtype=a_mat.dtype)
    rhs = jnp.concatenate([v * beta[..., None], kb * jnp.exp(gc)[..., None]], axis=-1)
    sol = lax.linalg.triangular_solve(lhs, rhs, left_side=True, lower=True, unit_diagonal=True)
    dv = v.shape[-1]
    u, w = sol[..., :dv], sol[..., dv:]
    qk = jnp.einsum('bhcid,bhcjd->bhcij', q, k) * decay
    qg = q * jnp.exp(gc)[..., None]
    kd = k * jnp.exp(gc[..., -1:] - gc)[..., None]
    g_last = jnp.exp(gc[..., -1])

    def step(S, xs):
        u_c, w_c, qk_c, qg_c, kd_c, gl_c = xs
        v_new = u_c - jnp.einsum('bhld,bhdv->bhlv', w_c, S)
        o_c = jnp.einsum('bhld,bhdv->bhlv', qg_c, S) + jnp.einsum('bhij,bhjv->bhiv', qk_c, v_new)
        S = S * gl_c[..., None, None] + jnp.einsum('bhld,bhlv->bhdv', kd_c, v_new)
        return S, o_c

    xs = tuple(jnp.moveaxis(a, 2, 0) for a in (u, w, qk, qg, kd, g_last))
    S, o = lax.scan(step, S0, xs)
    o = jnp.moveaxis(o, 0, 2).reshape(B, H, n_c * L, dv)[:, :, :T]
    return o, S

def _mlstm_chunked(q, k, v, ig, lf, C0, n0, m0):
    B, H, T, _ = q.shape
    L = min(T, CHUNK)
    n_c = -(-T // L)
    q, k, v, lf = (_pad_chunks(a, n_c, L, 0.0) for a in (q, k, v, lf))
    ig = _pad_chunks(ig, n_c, L, NEG)
    tril = jnp.tril(jnp.ones((L, L), bool))

    def step(carry, xs):
        C, n, m = carry
        q_c, k_c, v_c, i_c, f_c = xs
        b = jnp.cumsum(f_c, axis=-1)
        d_log = jnp.where(tril, b[..., :, None] - b[..., None, :] + i_c[..., None, :], NEG)
        inter = b + m[..., None]
        m_t = jnp.maximum(inter, d_log.max(axis=-1))
        s = jnp.einsum('bhid,bhjd->bhij', q_c, k_c) * jnp.exp(d_log - m_t[..., None])
        e_inter = jnp.exp(inter - m_t)
        num = e_inter[..., None] * jnp.einsum('bhld,bhdv->bhlv', q_c, C) + jnp.einsum('bhij,bhjv->bhiv', s, v_c)
        den = e_inter * jnp.einsum('bhld,bhd->bhl', q_c, n) + s.sum(axis=-1)
        h = num / jnp.maximum(jnp.abs(den), jnp.exp(-m_t))[..., None]
        m_new = m_t[..., -1]
        w_last = jnp.exp(b[..., -1:] - b + i_c - m_new[..., None])
        f_tot = jnp.exp(b[..., -1] + m - m_new)
        C = f_tot[..., None, None] * C + jnp.einsum('bhl,bhld,bhlv->bhdv', w_last, k_c, v_c)
        n = f_tot[..., None] * n + jnp.einsum('bhl,bhld->bhd', w_last, k_c)
        return (C, n, m_new), h

    xs = tuple(jnp.moveaxis(a, 2, 0) for a in (q, k, v, ig, lf))
    (C, n, m), h = lax.scan(step, (C0, n0, m0), xs)
    h = jnp.moveaxis(h, 0, 2).reshape(B, H, n_c * L, -1)[:, :, :T]
    return h, C, n, m

def _mixers(h, conv_buf, S0, C0, n0, m0, w_in, conv_w, gdn_a_log, gdn_dt_bias, gdn_norm_g,
            mlstm_i_bias, mlstm_f_bias, mlstm_norm_g):
    f32 = jnp.float32
    B, T, _ = h.shape
    proj = (h @ w_in).astype(f32)
    conv_in, z_a, a_a, b_a, q_b, k_b, v_b, o_b, i_b, f_b = _split(proj, SPLITS)
    xc = jnp.concatenate([conv_buf.astype(f32), conv_in], axis=1)
    cw = conv_w.astype(f32)
    conv = sum(xc[:, j:j + T] * cw[j] for j in range(CONV_W))
    new_conv = xc[:, T:]
    q_a, k_a, v_a = _split(jax.nn.silu(conv), (H_A * DK_A, H_A * DK_A, H_A * DV_A))
    q_a = _l2norm(_heads(q_a, H_A)) * DK_A ** -0.5
    k_a = _l2norm(_heads(k_a, H_A))
    v_a = _heads(v_a, H_A)
    g_a = -jnp.exp(gdn_a_log.astype(f32)) * jax.nn.softplus(a_a + gdn_dt_bias.astype(f32))
    beta_a = jax.nn.sigmoid(b_a)
    o_a, S = _gated_delta_rule(q_a, k_a, v_a, g_a.transpose(0, 2, 1), beta_a.transpose(0, 2, 1),
                               S0.astype(f32))
    o_a = _rms(o_a, gdn_norm_g) * jax.nn.silu(_heads(z_a, H_A))
    q_b = _heads(q_b, H_B) * DK_B ** -0.5
    k_b = _heads(k_b, H_B)
    v_b = _heads(v_b, H_B)
    ig = (i_b + mlstm_i_bias.astype(f32)).transpose(0, 2, 1)
    lf = jax.nn.log_sigmoid(f_b + mlstm_f_bias.astype(f32)).transpose(0, 2, 1)
    h_b, C, n, m = _mlstm_chunked(q_b, k_b, v_b, ig, lf, C0.astype(f32), n0.astype(f32), m0.astype(f32))
    h_b = _rms(h_b, mlstm_norm_g.reshape(H_B, 1, DV_B)) * jax.nn.sigmoid(_heads(o_b, H_B))
    mix = jnp.concatenate([_merge(o_a), _merge(h_b)], axis=-1).astype(h.dtype)
    return mix, new_conv, S, C, n, m

def _moe(x, router_w, router_b, w_gu, b_gu, w_down, b_down):
    B, T, D = x.shape
    n_tok = B * T
    xt = x.reshape(n_tok, D)
    logits = (xt @ router_w + router_b).astype(jnp.float32)
    top_val, top_idx = lax.top_k(logits, TOP_K)
    gates = jax.nn.softmax(top_val, axis=-1)
    n_slot = n_tok * TOP_K
    flat_e = top_idx.reshape(n_slot)
    flat_tok = jnp.repeat(jnp.arange(n_tok, dtype=jnp.int32), TOP_K)
    flat_g = gates.reshape(n_slot)
    counts = jnp.bincount(flat_e, length=N_EXPERTS)
    padded = (counts + MOE_BLOCK - 1) // MOE_BLOCK * MOE_BLOCK
    pad_end = jnp.cumsum(padded)
    pad_start = pad_end - padded
    start = jnp.cumsum(counts) - counts
    order = jnp.argsort(flat_e)
    e_sorted = flat_e[order]
    dest = pad_start[e_sorted] + jnp.arange(n_slot, dtype=jnp.int32) - start[e_sorted]
    n_blocks = -(-n_slot // MOE_BLOCK) + N_EXPERTS
    n_rows = n_blocks * MOE_BLOCK
    row_tok = jnp.full((n_rows,), n_tok, jnp.int32).at[dest].set(flat_tok[order])
    row_gate = jnp.zeros((n_rows,), jnp.float32).at[dest].set(flat_g[order])
    block_e = jnp.minimum(jnp.searchsorted(pad_end, jnp.arange(n_blocks, dtype=pad_end.dtype) * MOE_BLOCK,
                                           side='right'), N_EXPERTS - 1)
    x_rows = jnp.concatenate([xt, jnp.zeros((1, D), xt.dtype)], axis=0)[row_tok].reshape(n_blocks, MOE_BLOCK, D)

    def expert_block(args):
        xb, e = args
        hgu = xb @ w_gu[e] + b_gu[e]
        gate = jnp.minimum(hgu[:, :D_FF], SWIGLU_LIMIT)
        up = jnp.clip(hgu[:, D_FF:], -SWIGLU_LIMIT, SWIGLU_LIMIT)
        act = (up + 1.0) * gate * jax.nn.sigmoid(SWIGLU_ALPHA * gate)
        return act @ w_down[e] + b_down[e]

    y_rows = lax.map(expert_block, (x_rows, block_e)).reshape(n_rows, D)
    y = jax.ops.segment_sum(y_rows * row_gate[:, None].astype(y_rows.dtype), row_tok,
                            num_segments=n_tok + 1)[:n_tok]
    return y.reshape(B, T, D).astype(x.dtype)

def _trunk(x, p, conv_st, gdn_st, c_st, n_st, m_st, params):
    (norm_attn_g, w_in, conv_w, gdn_a_log, gdn_dt_bias, gdn_norm_g, mlstm_i_bias, mlstm_f_bias,
     mlstm_norm_g, w_out, norm_moe_g, router_w, router_b, expert_w_gu, expert_b_gu, expert_w_down,
     expert_b_down, norm_ple_g, ple_gate_w, ple_w, final_norm_g) = params
    new_conv, new_gdn, new_c, new_n, new_m = [], [], [], [], []
    for i in range(DEPTH):
        hn = _rms(x, norm_attn_g[i]).astype(x.dtype)
        mix, cv, S, C, n, m = _mixers(hn, conv_st[i], gdn_st[i], c_st[i], n_st[i], m_st[i], w_in[i], conv_w[i],
                                      gdn_a_log[i], gdn_dt_bias[i], gdn_norm_g[i], mlstm_i_bias[i],
                                      mlstm_f_bias[i], mlstm_norm_g[i])
        x = x + mix @ w_out[i]
        x = x + _moe(_rms(x, norm_moe_g[i]).astype(x.dtype), router_w[i], router_b[i], expert_w_gu[i],
                     expert_b_gu[i], expert_w_down[i], expert_b_down[i])
        gate = jax.nn.sigmoid(_rms(x, norm_ple_g[i]).astype(x.dtype) @ ple_gate_w[i])
        x = x + gate * (p[i] @ ple_w[i])
        new_conv.append(cv); new_gdn.append(S); new_c.append(C); new_n.append(n); new_m.append(m)
    y = _rms(x, final_norm_g).astype(x.dtype)
    return (y, jnp.stack(new_conv), jnp.stack(new_gdn), jnp.stack(new_c), jnp.stack(new_n), jnp.stack(new_m))

def setup_inputs(seed: int = 0) -> dict:
    key = jax.random.key(seed)
    ks = jax.random.split(key, 40)
    f32 = jnp.float32

    def nrm(k, shape, scale):
        return jax.random.normal(k, shape, f32) * scale

    def gain(k, shape):
        return 1.0 + 0.02 * jax.random.normal(k, shape, f32)

    dt = jnp.exp(jax.random.uniform(ks[9], (DEPTH, H_A), f32, np.log(0.001), np.log(0.1)))
    return {
        "x_prompt": nrm(ks[0], (BATCH, SEQ, D_MODEL), 1.0),
        "x_sample": nrm(ks[1], (DEC_BATCH, DEC_SEQ, D_MODEL), 1.0),
        "p_prompt": nrm(ks[2], (DEPTH, BATCH, SEQ, PLE_DIM), 1.0),
        "p_sample": nrm(ks[3], (DEPTH, DEC_BATCH, DEC_SEQ, PLE_DIM), 1.0),
        "state_conv": nrm(ks[4], (DEPTH, DEC_BATCH, CONV_W - 1, CONV_CH), 1.0),
        "state_gdn": nrm(ks[5], (DEPTH, DEC_BATCH, H_A, DK_A, DV_A), DK_A ** -0.5),
        "state_mlstm_c": nrm(ks[6], (DEPTH, DEC_BATCH, H_B, DK_B, DV_B), 0.1),
        "state_mlstm_n": nrm(ks[7], (DEPTH, DEC_BATCH, H_B, DK_B), 0.5),
        "state_mlstm_m": nrm(ks[8], (DEPTH, DEC_BATCH, H_B), 0.5),
        "norm_attn_g": gain(ks[10], (DEPTH, D_MODEL)),
        "w_in": nrm(ks[11], (DEPTH, D_MODEL, IN_W), D_MODEL ** -0.5),
        "conv_w": nrm(ks[12], (DEPTH, CONV_W, CONV_CH), CONV_W ** -0.5),
        "gdn_a_log": jnp.log(jax.random.uniform(ks[13], (DEPTH, H_A), f32, 1.0, 16.0)),
        "gdn_dt_bias": jnp.log(jnp.expm1(dt)),
        "gdn_norm_g": gain(ks[14], (DEPTH, DV_A)),
        "mlstm_i_bias": nrm(ks[15], (DEPTH, H_B), 0.1),
        "mlstm_f_bias": jax.random.uniform(ks[16], (DEPTH, H_B), f32, 3.0, 6.0),
        "mlstm_norm_g": gain(ks[17], (DEPTH, H_B * DV_B)),
        "w_out": nrm(ks[18], (DEPTH, D_MIX, D_MODEL), D_MIX ** -0.5),
        "norm_moe_g": gain(ks[19], (DEPTH, D_MODEL)),
        "router_w": nrm(ks[20], (DEPTH, D_MODEL, N_EXPERTS), D_MODEL ** -0.5),
        "router_b": nrm(ks[21], (DEPTH, N_EXPERTS), 0.01),
        "expert_w_gu": nrm(ks[22], (DEPTH, N_EXPERTS, D_MODEL, 2 * D_FF), D_MODEL ** -0.5),
        "expert_b_gu": nrm(ks[23], (DEPTH, N_EXPERTS, 2 * D_FF), 0.01),
        "expert_w_down": nrm(ks[24], (DEPTH, N_EXPERTS, D_FF, D_MODEL), D_FF ** -0.5),
        "expert_b_down": nrm(ks[25], (DEPTH, N_EXPERTS, D_MODEL), 0.01),
        "norm_ple_g": gain(ks[26], (DEPTH, D_MODEL)),
        "ple_gate_w": nrm(ks[27], (DEPTH, D_MODEL, D_MODEL), D_MODEL ** -0.5),
        "ple_w": nrm(ks[28], (DEPTH, PLE_DIM, D_MODEL), PLE_DIM ** -0.5),
        "final_norm_g": gain(ks[29], (D_MODEL,)),
    }

def reference(x_prompt, x_sample, p_prompt, p_sample, state_conv, state_gdn, state_mlstm_c, state_mlstm_n,
              state_mlstm_m, norm_attn_g, w_in, conv_w, gdn_a_log, gdn_dt_bias, gdn_norm_g, mlstm_i_bias,
              mlstm_f_bias, mlstm_norm_g, w_out, norm_moe_g, router_w, router_b, expert_w_gu, expert_b_gu,
              expert_w_down, expert_b_down, norm_ple_g, ple_gate_w, ple_w, final_norm_g):
    params = (norm_attn_g, w_in, conv_w, gdn_a_log, gdn_dt_bias, gdn_norm_g, mlstm_i_bias, mlstm_f_bias,
              mlstm_norm_g, w_out, norm_moe_g, router_w, router_b, expert_w_gu, expert_b_gu, expert_w_down,
              expert_b_down, norm_ple_g, ple_gate_w, ple_w, final_norm_g)
    B = x_prompt.shape[0]
    f32 = jnp.float32
    conv0 = jnp.zeros((DEPTH, B, CONV_W - 1, CONV_CH), f32)
    gdn0 = jnp.zeros((DEPTH, B, H_A, DK_A, DV_A), f32)
    c0 = jnp.zeros((DEPTH, B, H_B, DK_B, DV_B), f32)
    n0 = jnp.zeros((DEPTH, B, H_B, DK_B), f32)
    m0 = jnp.zeros((DEPTH, B, H_B), f32)
    y_prompt, conv_p, gdn_p, c_p, n_p, m_p = _trunk(x_prompt, p_prompt, conv0, gdn0, c0, n0, m0, params)
    y_sample, conv_s, gdn_s, c_s, n_s, m_s = _trunk(x_sample, p_sample, state_conv, state_gdn, state_mlstm_c,
                                                    state_mlstm_n, state_mlstm_m, params)
    return (y_prompt, y_sample, conv_p, gdn_p, c_p, n_p, m_p, conv_s, gdn_s, c_s, n_s, m_s)


_drawn_inputs = setup_inputs


def setup_inputs(seed=0):
    import zlib

    import numpy as np

    out = dict(_drawn_inputs(seed))
    spreads = {}
    factors = {'gdn_norm_g': 3.056,
     'mlstm_i_bias': 10.415,
     'mlstm_norm_g': 3.075,
     'router_b': 2.946,
     'expert_b_gu': 8.0,
     'expert_b_down': 8.0,
     'norm_ple_g': 200.0,
     'final_norm_g': 25.154}
    for name, (base, spread) in spreads.items():
        noise = np.random.default_rng([zlib.crc32(name.encode()), seed]).standard_normal(out[name].shape)
        drawn = base * np.exp(spread * noise) if base else spread * noise
        out[name] = __import__('jax').numpy.asarray(drawn.astype(out[name].dtype))
    for name, factor in factors.items():
        out[name] = (out[name] * factor).astype(out[name].dtype)
    return out
```

```python
from contextlib import ExitStack

import concourse.bass as bass
from concourse import mybir

F32 = mybir.dt.float32
I32 = mybir.dt.int32
ALU = mybir.AluOpType
ACT = mybir.ActivationFunctionType
AX = mybir.AxisListType.X

P = 128
D = 1024
KD = D // P
FF = 1024
H = 4
DK = 128
DQ = 64
CW = 4
NCH = 12
NSEQ = 8
LS = 8
TP = 256
NTOK = TP + NSEQ * LS
ROWS = [128, 128, 64]
OFF = [0, 128, 256]
NE = 32
TOPK = 4
PLE = 256
EPS = 1e-6
NEG = -1e30
LIMIT = 7.0
ALPHA = 1.702
SL = 64
NOV = 24
NB = NE + NOV
SLOTW = 2048
NGU = 8
NDN = 4
NSLOT = NGU + NDN
XCW = CW - 1 + TP
XCS = CW - 1 + LS
XC = XCW + NSEQ * XCS
C_Z, C_AB, C_QB, C_VB, C_OB, C_IF = 1536, 2048, 2056, 2568, 3080, 3592


def bc(ap, axis, n):
    v = ap.unsqueeze(axis)
    shape = list(v.shape)
    shape[axis] = n
    return v.to_broadcast(shape)


def build(nc, a, o):
    with ExitStack() as ctx:
        sems = {}

        def sb(name, shape, dt=F32):
            return ctx.enter_context(nc.sbuf_tensor(name, shape, dt))

        def sem(name):
            if name not in sems:
                sems[name] = ctx.enter_context(nc.semaphore(name))
            return sems[name]

        ring = sb("ring", [P, NSLOT * SLOTW])
        X = sb("X", [P, 3, D])
        XS = sb("XS", [P, 3, D])
        xT = sb("xT", [P, KD, NTOK])
        szo = sb("szo", [P, 8, NTOK])
        qm = sb("qm", [P, H, NTOK])
        kp = sb("kp", [P, 2, NTOK])
        va = sb("va", [P, 3, H, DK + 1])
        SC = sb("SC", [P, 15, H * P])
        ident = sb("ident", [P, P])
        ones = sb("ones", [P, P])
        upto = sb("upto", [P, P])
        upto_s = sb("upto_s", [64, 64])
        before = sb("before", [P, P])
        seg_s = sb("seg_s", [64, 64])
        negU = sb("negU", [P, P])
        negU_s = sb("negU_s", [64, 64])
        negL = sb("negL", [P, P])
        negL_s = sb("negL_s", [64, 64])
        lastr = sb("lastr", [P, P])
        lastr_s = sb("lastr_s", [64, 64])
        inds = sb("inds", [64, NSEQ])
        lasts = sb("lasts", [64, NSEQ])
        lvl = sb("lvl", [P, 7, P])
        iota_i = sb("iota_i", [P, SL], I32)
        iota_s = sb("iota_s", [P, SL])
        prow = sb("prow", [77, P])
        pcol = sb("pcol", [P, 77])
        bc16 = sb("bc16", [P, 16])
        rbias = sb("rbias", [P, NE])
        g16 = sb("g16", [P, 3, 16])
        z8 = sb("z8", [P, 3, 8])
        t8 = sb("t8", [P, 3, 8])
        gl8 = sb("gl8", [P, 3, 8])
        coef = sb("coef", [P, 8])
        beta = sb("beta", [P, 3, H])
        igc = sb("igc", [P, 3, H])
        gcb = sb("gcb", [P, 3, 8])
        gto = sb("gto", [P, 3, 8])
        ex = sb("ex", [P, 3, 12])
        kco = sb("kco", [P, 3, H])
        glx = sb("glx", [64, NSEQ, 8])
        egx = sb("egx", [P, NSEQ, 8])
        ms = sb("ms", [P, 3, 12, H])
        st = sb("st", [P, 3, 2, H])
        fx = sb("fx", [64, NSEQ, H])
        ftp = sb("ftp", [P, NSEQ, 2])
        qnx = sb("qnx", [64, H, NSEQ])
        nst = sb("nst", [P, 4, 3])
        mhalf = sb("mhalf", [P, 1])
        epsc = sb("epsc", [P, 2])
        bgu = sb("bgu", [P, 16, NE])
        bdn = sb("bdn", [P, KD, NE])
        w16 = sb("w16", [P, KD, 16])
        rw = sb("rw", [P, KD, NE])
        lg = sb("lg", [P, 3, NE])
        posb = sb("posb", [P, 3, NB])
        gateb = sb("gateb", [P, 3, NB])
        etabf = sb("etabf", [P, NB])
        etab = sb("etab", [P, NB], I32)
        ntotf = sb("ntotf", [P, 1])
        ntot = sb("ntot", [P, 1], I32)
        MPREV, MCUM, MT, MNEW, DEN, RDEN, EINT, EMT, WL, FT = range(10)

        PB = [ctx.enter_context(nc.psum_tensor(f"bank{i}", [P, 512], F32)) for i in range(8)]

        at = 0

        def take(n):
            nonlocal at
            at += n
            return ring[:, at - n:at]

        xcf = take(NCH * XC)
        xc = xcf.rearrange("p (c t) -> p c t", c=NCH)
        qkv = take(NCH * NTOK).rearrange("p (c t) -> p c t", c=NCH)
        S = take(NSEQ * H * DK).rearrange("p (s h v) -> p s h v", s=NSEQ, h=H)
        Cs = take(NSEQ * 2 * (DK + 1)).rearrange("p (s q v) -> p s q v", s=NSEQ, q=2)
        Sp = take(H * DK).rearrange("p (h v) -> p h v", h=H)
        Cp = take(2 * (DK + 1)).rearrange("p (q v) -> p q v", q=2)
        assert at <= NGU * SLOTW
        wbuf = [ring[:, (8 + 2 * i) * SLOTW:(10 + 2 * i) * SLOTW].rearrange("p (k n) -> p k n", k=KD) for i in range(2)]
        wo = ring[:, 8 * SLOTW:12 * SLOTW].rearrange("p (k n) -> p k n", k=KD)
        wple = ring[:, 0:4 * SLOTW].rearrange("p (k n) -> p k n", k=KD)
        fgain = ring[:, 4 * SLOTW:4 * SLOTW + D]
        srow = ring[:, 10 * SLOTW:11 * SLOTW]
        xs = XS[:, :, :].rearrange("p t d -> p (t d)")
        vexp = [xs[0:64, i * NSEQ * 129:(i + 1) * NSEQ * 129].rearrange("p (s v) -> p s v", s=NSEQ) for i in range(2)]
        crow = xcf[0:27, 0:NCH * P]
        scf = SC[:, :, :].rearrange("p b x -> p (b x)")

        def buf(i):
            return SC[:, i, :].rearrange("p (h x) -> p h x", h=H)

        B_DG, B_ED, B_P1, B_A, B_T, B_W, B_Y, B_QK, B_VB, B_KBG, B_KD, B_WT, B_VN, B_O, B_ST = (buf(i) for i in range(15))
        stage = SC[:, 14, :]
        M_DG, M_P, M_S, M_ST, M_KW = B_P1, B_A, B_T, B_W, B_Y
        M_NUM = scf[:, 8 * 512:8 * 512 + H * 129].rearrange("p (h v) -> p h v", h=H)

        e_at = 0

        def etake(n):
            nonlocal e_at
            e_at += n
            assert e_at <= 15 * 512
            return scf[:, e_at - n:e_at]

        SEL = etake(3 * SL).rearrange("p (t s) -> p t s", t=3)
        SELG = etake(3 * SL).rearrange("p (t s) -> p t s", t=3)
        SELT = etake(3 * P)
        xg = etake(KD * SL).rearrange("p (k s) -> p k s", k=KD)
        gt = etake(KD * SL).rearrange("p (k s) -> p k s", k=KD)
        ut = etake(KD * SL).rearrange("p (k s) -> p k s", k=KD)
        sg = etake(KD * SL).rearrange("p (k s) -> p k s", k=KD)
        act_t = etake(KD * SL).rearrange("p (k s) -> p k s", k=KD)
        ye = etake(KD * SL).rearrange("p (k s) -> p k s", k=KD)
        yT = etake(D)
        tb = [scf[:, 1024 * i:1024 * i + NOV * NE].rearrange("p (j e) -> p j e", j=NOV) for i in range(4)]
        t3 = [scf[:, 4096 + 128 * i:4096 + 128 * i + 3 * NE].rearrange("p (t e) -> p t e", t=3) for i in range(10)]
        t1 = [scf[:, 6144 + 64 * i:6144 + 64 * i + NE] for i in range(12)]
        pw = scf[:, 0:3 * D].rearrange("p (t d) -> p t d", t=3)
        gsc = [scf[:, 3 * D + 512 * i:3 * D + 512 * (i + 1)] for i in range(2)]
        szf = szo[:, :, :].rearrange("p c t -> p (c t)")
        plw = szf[:, 0:2048].rearrange("p (k n) -> p k n", k=2)
        qmf = qm[:, :, :].rearrange("p c t -> p (c t)")
        pT = qmf[:, 0:2 * NTOK].rearrange("p (k t) -> p k t", k=2)
        ptk = va[:, :, :, :].rearrange("p t h v -> p (t h v)")[:, 0:3 * PLE].rearrange("p (t d) -> p t d", t=3)

        x_in = [a["x_prompt"].rearrange("b t d -> (b t) d"), a["x_sample"].rearrange("b t d -> (b t) d")]
        p_in = [a["p_prompt"].rearrange("o b t d -> (o b t) d"), a["p_sample"].rearrange("o b t d -> (o b t) d")]
        y_out = [o["y_p"].rearrange("b t d -> (b t) d"), o["y_s"].rearrange("b t d -> (b t) d")]

        def tok_dram(pair, t):
            return pair[0][OFF[t]:OFF[t] + P, :] if t < 2 else pair[1]

        w_in = a["w_in"].rearrange("o (k p) n -> p (o k) n", p=P)
        w_out = a["w_out"].rearrange("o (k p) n -> p (o k) n", p=P)
        w_gu = a["expert_w_gu"].rearrange("o e (k p) n -> (o e) p k n", p=P)
        w_dn = a["expert_w_down"].rearrange("o e (k p) n -> (o e) p k n", p=P)

        def slot(c):
            return ring[:, c * SLOTW:(c + 1) * SLOTW]

        def load_chunk(eng, e, c):
            if c < NGU:
                src, dst = w_gu[e, :, c, :], slot(c)
            else:
                k = 2 * (c - NGU)
                src, dst = w_dn[e, :, k:k + 2, :], slot(c).rearrange("p (k n) -> p k n", k=2)
            eng.dma_start(dst, src).then_inc(sem(f"w_full{c}"), 16)

        GROUPS = [("k", 512), ("q", 0), ("v", 1024), ("qkb", C_QB), ("vb", C_VB), ("z", C_Z), ("ob", C_OB)]
        NG = len(GROUPS)
        PROD = [(g, c) for g in range(NG) for c in range(3 if GROUPS[g][0] == "vb" else 4)]

        block = ctx.enter_context(nc.Block())

        @block.sync
        def _(sp):
            for t in range(3):
                sp.dma_start(X[0:ROWS[t], t, :], tok_dram(x_in, t)).then_inc(sem("x_in"), 16)
            rows = [("norm_attn_g", 0, 8), ("norm_moe_g", 8, 8), ("norm_ple_g", 16, 8), ("conv_w", 24, 48),
                    ("gdn_norm_g", 72, 1), ("mlstm_norm_g", 73, 4)]
            for name, r, n in rows:
                src = a[name].rearrange("o w (c p) -> (o w c) p", p=P) if name == "conv_w" else \
                    a[name].rearrange("o (c p) -> (o c) p", p=P)
                sp.dma_start(prow[r:r + n, :], src).then_inc(sem("params_in"), 16)
            for i, name in enumerate(["gdn_a_log", "gdn_dt_bias", "mlstm_i_bias", "mlstm_f_bias"]):
                sp.dma_start(bc16[:, 4 * i:4 * i + 4], a[name].to_broadcast([P, 4])).then_inc(sem("bc_in"), 16)
            sp.dma_start(w16[:, :, 0:8], w_in[:, :, C_AB:C_AB + 8]).then_inc(sem("w16_in"), 16)
            sp.dma_start(w16[:, :, 8:16], w_in[:, :, C_IF:C_IF + 8]).then_inc(sem("w16_in"), 16)
            sp.dma_start(srow[0:24, 0:1536], a["state_conv"].rearrange("o b w c -> (o b w) c")).then_inc(sem("rows_in"), 16)
            sp.dma_start(srow[32:64, 0:2048], a["expert_b_gu"].rearrange("o e n -> (o e) n")).then_inc(sem("rows_in"), 16)
            sp.dma_start(srow[64:96, 0:1024], a["expert_b_down"].rearrange("o e n -> (o e) n")).then_inc(sem("rows_in"), 16)
            for g, (_, c0) in enumerate(GROUPS):
                if g == 1:
                    sp.wait_ge(sem("rows_used"), 1)
                if g >= 2:
                    sp.wait_ge(sem("proj"), sum(x < g - 1 for x, _ in PROD))
                sp.dma_start(wbuf[g % 2], w_in[:, :, c0:c0 + 512]).then_inc(sem(f"group_in{g % 2}"), 16)
                if g == 1:
                    sp.wait_ge(sem("consts1"), 1)
                    for s in range(NSEQ):
                        sp.dma_start(S[:, s, :, :], a["state_gdn"][0, s].rearrange("h k v -> k h v")).then_inc(sem("S_in"), 16)
                        sp.dma_start(ms[LS * s:LS * s + LS, 2, MPREV, :], a["state_mlstm_m"][0, s:s + 1, :].to_broadcast([LS, H]))\
                            .then_inc(sem("m_in"), 16)
                        for q in range(2):
                            sp.dma_start(Cs[:, s, q, 0:DK], a["state_mlstm_c"][0, s, 2 * q:2 * q + 2].rearrange("h k v -> (h k) v"))\
                                .then_inc(sem("C_in"), 16)
                            sp.dma_start(Cs[:, s, q, DK:DK + 1], a["state_mlstm_n"][0, s, 2 * q:2 * q + 2, :]
                                         .rearrange("h (k u) -> (h k) u", u=1)).then_inc(sem("C_in"), 16)
                    sp.dma_start(rbias[:, :], a["router_b"].to_broadcast([P, NE])).then_inc(sem("rw_in"), 16)
                    sp.dma_start(rw[:, :, :], a["router_w"].rearrange("o (k p) n -> p (o k) n", p=P)).then_inc(sem("rw_in"), 16)
            sp.wait_ge(sem("proj"), len(PROD))
            sp.dma_start(wo, w_out).then_inc(sem("wo_in"), 16)
            nout = 0

            def store(dst, src):
                nonlocal nout
                nout += 1
                sp.dma_start(dst, src).then_inc(sem("out"), 16)

            sp.wait_ge(sem("crow"), NCH)
            store(o["conv_p"].rearrange("o b w c -> (o b w) c"), crow[0:3, :])
            store(o["conv_s"].rearrange("o b w c -> (o b w) c"), crow[3:27, :])
            sp.wait_ge(sem("Sp_done"), 2)
            store(o["gdn_p"][0, 0].rearrange("h k v -> k h v"), Sp)
            sp.wait_ge(sem("Cp_done"), 2)
            for q in range(2):
                store(o["c_p"][0, 0, 2 * q:2 * q + 2].rearrange("h k v -> (h k) v"), Cp[:, q, 0:DK])
                store(o["n_p"][0, 0, 2 * q:2 * q + 2].rearrange("h (k u) -> (h k) u", u=1), Cp[:, q, DK:DK + 1])
            sp.wait_ge(sem("mnew"), 3)
            store(o["m_p"][0], ms[0:1, 1, MNEW, :])
            for s in range(NSEQ):
                store(o["m_s"][0, s:s + 1, :], ms[LS * s:LS * s + 1, 2, MNEW, :])
            sp.wait_ge(sem("Ss_done"), H)
            sp.wait_ge(sem("Cs_done"), 2)
            for s in range(NSEQ):
                store(o["gdn_s"][0, s].rearrange("h k v -> k h v"), S[:, s, :, :])
                for q in range(2):
                    store(o["c_s"][0, s, 2 * q:2 * q + 2].rearrange("h k v -> (h k) v"), Cs[:, s, q, 0:DK])
                    store(o["n_s"][0, s, 2 * q:2 * q + 2].rearrange("h (k u) -> (h k) u", u=1), Cs[:, s, q, DK:DK + 1])
            sp.wait_ge(sem("out"), 16 * nout)
            sp.wait_ge(sem("x1"), 6)
            for c in range(NSLOT):
                load_chunk(sp, 0, c)
            sp.dma_start(plw, a["ple_w"].rearrange("o (k p) n -> p (o k) n", p=P)).then_inc(sem("plw_in"), 16)
            for t in range(3):
                sp.dma_start(ptk[0:ROWS[t], t, :], tok_dram(p_in, t)).then_inc(sem("p_in"), 16)
            sp.wait_ge(sem("tables"), 1)
            total = sp.value_load(ntot[0:1, 0:1], min_val=NE, max_val=NB - 1)
            with sp.Fori(1, total) as b:
                e = sp.value_load(etab[0:1, bass.ds(b, 1)], min_val=0, max_val=NE - 1)
                for c in range(NSLOT):
                    sp.wait_ge(sem("w_used"), NSLOT * b - NSLOT + c + 1)
                    load_chunk(sp, e, c)
            sp.wait_ge(sem("moe_done"), 1)
            sp.dma_start(wple, a["ple_gate_w"].rearrange("o (k p) n -> p (o k) n", p=P)).then_inc(sem("wple_in"), 16)
            sp.dma_start(fgain, a["final_norm_g"].rearrange("(o d) -> o d", o=1).to_broadcast([P, D])).then_inc(sem("fg_in"), 16)
            for t in range(3):
                sp.wait_ge(sem("y_ready"), t + 1)
                store(y_out[0][OFF[t]:OFF[t] + P, :] if t < 2 else y_out[1], X[0:ROWS[t], t, :])
            sp.wait_ge(sem("out"), 16 * nout)

        @block.gpsimd
        def _(pool):
            n = [0]

            def link(ins):
                n[0] += 1
                ins.then_inc(sem("pool_chain"), 1)
                pool.wait_ge(sem("pool_chain"), n[0])

            def keep(ap, pattern, base, cm, fill, op=ALU.is_ge):
                link(nc.gpsimd.affine_select(out=ap, in_=ap, compare_op=op, fill=fill, base=base, pattern=pattern,
                                             channel_multiplier=cm))

            def fill(ap, v):
                link(nc.gpsimd.memset(ap, v))

            fill(ident[:], 0.0)
            keep(ident[:], [[-1, P]], 0, 1, 1.0, ALU.not_equal)
            nc.gpsimd.memset(ones[:], 1.0).then_inc(sem("consts0"), 1)
            fill(epsc[:, 0:1], EPS)
            fill(epsc[:, 1:2], float(DK) * EPS)
            fill(mhalf[:], -0.5)
            fill(xc[:, :, 0:CW - 1], 0.0)
            fill(va[:, :, :, DK:DK + 1], 1.0)
            fill(qm[:], 0.0)
            fill(g16[:], 0.0)
            fill(gcb[:], 0.0)
            fill(gto[:], 0.0)
            fill(nst[:], 1.0)
            fill(lg[:], 0.0)
            nc.gpsimd.memset(ms[:], 0.0).then_inc(sem("consts1"), 1)

            def rsqrt(ready, count, done, out, in_):
                pool.wait_ge(sem(ready), count)
                sh = list(in_.shape)
                e = mhalf[0:sh[0], :] if len(sh) == 2 else None
                nc.gpsimd.tensor_tensor(out, in_, e.to_broadcast(sh), ALU.pow).then_inc(sem(done), 1)

            rsqrt("ms", 1, "rs", nst[:, 2, :], nst[:, 1, :])

            def segments(ap, cols=False):
                v = ap if cols else ap.rearrange("p (s i) -> p s i", s=NSEQ)
                z = [] if cols else [[0, LS]]
                keep(v, [[-LS, NSEQ]] + z, 0, 1, 0.0)
                keep(v, [[LS, NSEQ]] + z, LS - 1, -1, 0.0)

            fill(upto[:], 1.0)
            keep(upto[:], [[1, P]], 0, -1, 0.0)
            fill(seg_s[:], 1.0)
            segments(seg_s[:])
            fill(inds[:], 1.0)
            segments(inds[:], True)
            link(nc.gpsimd.tensor_tensor(upto_s[:], upto[0:64, 0:64], seg_s[:], ALU.mult))
            fill(before[:], 1.0)
            keep(before[:], [[1, P]], -1, -1, 0.0)
            fill(negU[:], 0.0)
            keep(negU[:], [[1, P]], 0, -1, NEG)
            link(nc.gpsimd.tensor_scalar(negU_s[:], upto_s[:], -1.0, -NEG, ALU.add, ALU.mult))
            fill(negL[:], 0.0)
            keep(negL[:], [[-1, P]], 0, 1, NEG)
            link(nc.gpsimd.tensor_scalar(negL_s[:], seg_s[:], -1.0, -NEG, ALU.add, ALU.mult))
            keep(negL_s[:], [[-1, 64]], 0, 1, NEG)
            fill(lastr[:], 1.0)
            keep(lastr[:], [[0, P]], -(P - 1), 1, 0.0)
            fill(lasts[:], 0.0)
            keep(lasts[:], [[-LS, NSEQ]], -(LS - 1), 1, 1.0, ALU.not_equal)
            fill(lastr_s[:], 0.0)
            keep(lastr_s[:].rearrange("p (s i) -> p s i", s=NSEQ), [[-LS, NSEQ], [0, LS]], -(LS - 1), 1, 1.0, ALU.not_equal)
            fill(lvl[:], 0.0)
            for l in range(7):
                s = 1 << l
                nb = P // (2 * s)
                v = lvl[:, l, :].rearrange("p (b x) -> p b x", b=nb)[:, :, s:2 * s]
                fill(v, 1.0)
                keep(v, [[-2 * s, nb], [0, s]], 0, 1, 0.0)
                keep(v, [[2 * s, nb], [0, s]], s - 1, -1, 0.0)
            link(nc.gpsimd.iota(iota_i[:], [[1, SL]], base=0, channel_multiplier=0))
            nc.gpsimd.tensor_copy(iota_s[:], iota_i[:]).then_inc(sem("consts2"), 1)
            order = [4, 5, 6, 7, 0, 1, 2, 3]
            pool.wait_ge(sem("xsT"), 6)
            for i, c in enumerate(order):
                pool.wait_ge(sem("silu"), i + 1)
                if i >= 2:
                    pool.wait_ge(sem("nrm"), i - 1)
                nc.gpsimd.tensor_tensor(XS[:, i % 2, 0:NTOK], qkv[:, c, :], qkv[:, c, :], ALU.mult).then_inc(sem("sq"), 1)
            for c in range(8):
                pool.wait_ge(sem("szo"), c + 1)
                gain = pcol[:, 72:73] if c < 4 else pcol[:, 69 + c:70 + c]
                nc.gpsimd.tensor_scalar(szo[:, c, :], szo[:, c, :], gain, None, ALU.mult).then_inc(sem("szg"), 1)
            for t in range(3):
                for i in range(2):
                    R = ROWS[t]
                    rsqrt("hms", 2 * t + i + 1, "hrs", ms[0:R, t, 10 + i, :], st[0:R, t, i, :])
            rsqrt("ms", 2, "rs", nst[:, 2, :], nst[:, 1, :])
            rsqrt("ms", 3, "rs", nst[:, 2, :], nst[:, 1, :])
            for t in range(3):
                rsqrt("ms", 4 + t, "rs", nst[0:ROWS[t], 2, t:t + 1], nst[0:ROWS[t], 1, t:t + 1])

        @block.tensor
        def _(pe):
            mm = nc.tensor.matmul
            turn = nc.tensor.transpose

            def bank(b, R, h, w):
                return PB[b][0:R, h * P:h * P + w]

            pe.wait_ge(sem("consts0"), 1)
            pe.wait_ge(sem("params_in"), 16 * 6)
            turn(PB[0][:, 0:77], prow[:, :], ident[0:77, 0:77]).then_inc(sem("pcolT"), 1)
            pe.wait_ge(sem("rows_in"), 16 * 3)
            for c in range(NCH):
                turn(PB[1][:, 24 * c:24 * c + 24], srow[0:24, c * P:c * P + P], ident[0:24, 0:24])
            for c in range(16):
                turn(PB[2][:, NE * c:NE * c + NE], srow[32:64, c * P:c * P + P], ident[32:64, 32:64])
            for c in range(KD):
                last = turn(PB[3][:, NE * c:NE * c + NE], srow[64:96, c * P:c * P + P], ident[64:96, 64:96])
            last.then_inc(sem("rows_used"), 1)

            def turn_x(nth, b0):
                for t in range(3):
                    R = ROWS[t]
                    pe.wait_ge(sem("xs"), 3 * nth + t + 1)
                    for hb in range(2):
                        i = 2 * t + hb
                        if i >= 2:
                            pe.wait_ge(sem("xT"), 6 * nth + i - 1)
                        for k in range(4):
                            c = 4 * hb + k
                            last = turn(PB[b0 + i % 2][:, k * P:k * P + R], XS[0:R, t, c * P:c * P + P], ident[0:R, 0:R])
                        last.then_inc(sem("xsT"), 1)

            turn_x(0, 4)
            pe.wait_ge(sem("xT"), 6)
            pe.wait_ge(sem("w16_in"), 32)
            pe.wait_ge(sem("pcol"), 1)
            for t in range(3):
                R = ROWS[t]
                for k in range(KD):
                    last = mm(PB[0][0:R, 16 * t:16 * t + 16], xT[:, k, OFF[t]:OFF[t] + R], w16[:, k, :],
                              start=(k == 0), stop=(k == KD - 1))
            last.then_inc(sem("g16_ps"), 1)
            for j, (g, c) in enumerate(PROD):
                if c == 0:
                    pe.wait_ge(sem(f"group_in{g % 2}"), 16 * (g // 2 + 1))
                if j >= 4:
                    pe.wait_ge(sem("proj_out"), j - 3)
                w = wbuf[g % 2]
                for k in range(KD):
                    if GROUPS[g][0] == "vb":
                        last = mm(PB[4 + j % 4][0:ROWS[c], :], xT[:, k, OFF[c]:OFF[c] + ROWS[c]], w[:, k, :],
                                  start=(k == 0), stop=(k == KD - 1))
                    else:
                        last = mm(PB[4 + j % 4][:, 0:NTOK], w[:, k, c * P:c * P + P], xT[:, k, :],
                                  start=(k == 0), stop=(k == KD - 1))
                last.then_inc(sem("proj"), 1)
            pe.wait_ge(sem("rows_out"), 3)
            for i in range(8):
                pe.wait_ge(sem("sq"), i + 1)
                if i >= 2:
                    pe.wait_ge(sem("nrm_out"), i - 1)
                mm(PB[1 + i % 2][:, 0:NTOK], ones[:], XS[:, i % 2, 0:NTOK], start=True, stop=True).then_inc(sem("nrm"), 1)
            pe.wait_ge(sem("cnew"), 1)
            pe.wait_ge(sem("proj_out"), len(PROD))
            for c in range(NCH):
                if c % 4 == 0:
                    if c:
                        pe.wait_ge(sem("crow"), c)
                turn(bank(4, 27, c % 4, P), SC[:, 14, 27 * c:27 * c + 27], ident[:]).then_inc(sem("cnewT"), 1)
            pe.wait_ge(sem("gl8"), 1)
            pe.wait_ge(sem("consts2"), 1)
            for t in range(3):
                R = ROWS[t]
                mm(PB[0][0:R, 8 * t:8 * t + 8], upto[:] if t < 2 else upto_s[:], gl8[0:R, t, :], start=True, stop=True)
                mm(PB[0][0:R, 32 + 8 * t:40 + 8 * t], ones[:] if t < 2 else seg_s[:], gl8[0:R, t, :], start=True, stop=True)
            mm(PB[0][:, 64:128], ones[0:64, :], glx[:].rearrange("p s g -> p (s g)"), start=True, stop=True)\
                .then_inc(sem("cum"), 1)
            pe.wait_ge(sem("cum_out"), 1)
            pe.wait_ge(sem("crow"), NCH)
            pe.wait_ge(sem("qkn"), 8)
            pe.wait_ge(sem("silu"), NCH)

            levels = 0
            for t in range(3):
                R, o0 = ROWS[t], OFF[t]
                tk = slice(o0, o0 + R)
                if t > 0:
                    pe.wait_ge(sem("mix"), 2 * t)
                pe.wait_ge(sem("diag"), 2 * t + 1)
                mm(PB[0][0:R, 0:4 * R], ones[0:R, 0:R], B_DG[0:R, :, 0:R], start=True, stop=True).then_inc(sem("R_ps"), 1)
                for h in range(H):
                    last = mm(bank(1, R, h, R), qkv[:, 4 + h, tk], qkv[:, 4 + h, tk], start=True, stop=True)
                last.then_inc(sem("kqv_ps"), 1)
                for h in range(H):
                    last = mm(bank(2, R, h, R), qkv[:, 4 + h, tk], qkv[:, h, tk], start=True, stop=True)
                last.then_inc(sem("kqv_ps"), 1)
                for h in range(H):
                    last = turn(bank(3, R, h, P), qkv[:, 4 + h, tk], ident[:])
                last.then_inc(sem("kqv_ps"), 1)
                for h in range(H):
                    last = turn(bank(4, R, h, P), qkv[:, 8 + h, tk], ident[:])
                last.then_inc(sem("kqv_ps"), 1)
                pe.wait_ge(sem("P1"), t + 1)
                for h in range(H):
                    last = turn(bank(5, R, h, R), B_P1[0:R, h, 0:R], ident[0:R, 0:R])
                last.then_inc(sem("A_ps"), 1)
                pe.wait_ge(sem("A"), t + 1)
                nl = 7 if t < 2 else 3
                for l in range(nl):
                    if l > 0:
                        pe.wait_ge(sem("TW"), levels)
                    levels += 1
                    Tl = [ident[0:R, 0:R] if l == 0 else B_T[0:R, h, 0:R] for h in range(H)]
                    Wl = [ident[0:R, 0:R] if l == 0 else B_W[0:R, h, 0:R] for h in range(H)]
                    for h in range(H):
                        last = mm(bank(5, R, h, R), B_A[0:R, h, 0:R], Wl[h], start=True, stop=True)
                    last.then_inc(sem("Y_ps"), 1)
                    pe.wait_ge(sem("Y"), levels)
                    for h in range(H):
                        mm(bank(6, R, h, R), B_Y[0:R, h, 0:R], Tl[h], start=True, stop=True)
                    for h in range(H):
                        last = mm(bank(7, R, h, R), Tl[h], B_Y[0:R, h, 0:R], start=True, stop=True)
                    last.then_inc(sem("TW_ps"), 1)
                pe.wait_ge(sem("TW"), levels)
                for h in range(H):
                    last = mm(bank(5, R, h, P), B_W[0:R, h, 0:R], B_VB[0:R, h, :], start=True, stop=True)
                last.then_inc(sem("u_ps"), 1)
                if t > 0:
                    for h in range(H):
                        last = mm(bank(6, P, h, R), B_KBG[0:R, h, :], B_W[0:R, h, 0:R], start=True, stop=True)
                    last.then_inc(sem("wT_ps"), 1)
                    pe.wait_ge(sem("wT"), t)
                if t == 1:
                    for h in range(H):
                        mm(bank(7, R, h, P), B_WT[:, h, 0:R], Sp[:, h, :], start=True, stop=True)
                    for h in range(H):
                        last = mm(bank(6, R, h, P), qkv[:, h, tk], Sp[:, h, :], start=True, stop=True)
                    last.then_inc(sem("wqS_ps"), 1)
                if t == 2:
                    pe.wait_ge(sem("S_in"), 16 * NSEQ)
                    for h in range(H):
                        for s in range(NSEQ):
                            c = 64 * h + LS * s
                            mm(PB[7][:, c:c + LS], S[:, s, h, :], B_WT[:, h, LS * s:LS * s + LS], start=True, stop=True)
                            last = mm(PB[7][:, 256 + c:256 + c + LS], S[:, s, h, :],
                                      qkv[:, h, o0 + LS * s:o0 + LS * s + LS], start=True, stop=True)
                    last.then_inc(sem("wqST_ps"), 1)
                    pe.wait_ge(sem("wqST"), 1)
                    for h in range(H):
                        turn(bank(7, R, h, P), stage[:, 64 * h:64 * h + 64], ident[:])
                    for h in range(H):
                        last = turn(bank(6, R, h, P), stage[:, 256 + 64 * h:256 + 64 * h + 64], ident[:])
                    last.then_inc(sem("wqS_ps"), 1)
                pe.wait_ge(sem("vnew"), t + 1)
                for h in range(H):
                    last = mm(bank(1, R, h, P), B_QK[0:R, h, 0:R], B_VN[0:R, h, :], start=True, stop=True)
                last.then_inc(sem("o_ps"), 1)
                if t < 2:
                    for h in range(H):
                        last = mm(bank(2, P, h, P), B_KD[0:R, h, :], B_VN[0:R, h, :], start=True, stop=True)
                    last.then_inc(sem("dS_ps"), 1)
                else:
                    for h in range(H):
                        pe.wait_ge(sem("vx"), h + 1)
                        if h > 0:
                            pe.wait_ge(sem("Ss_done"), h)
                        for n in range(2):
                            last = mm(PB[2 + n][:, :], B_KD[0:R, h, :], vexp[h % 2][0:R, 4 * n:4 * n + 4, 0:DK],
                                      start=True, stop=True)
                        last.then_inc(sem("dS_ps"), 1)
                pe.wait_ge(sem("on"), t + 1)
                for h in range(H):
                    last = turn(bank(0, P, h, R), B_DG[0:R, h, :], ident[0:R, 0:R])
                last.then_inc(sem("mixT_ps"), 1)
                pe.wait_ge(sem("diag"), 2 * t + 2)
                mm(PB[4][0:R, 0:4 * R], ones[0:R, 0:R], M_DG[0:R, :, 0:R], start=True, stop=True).then_inc(sem("C_ps"), 1)
                for h in range(H):
                    last = mm(bank(5, R, h, R), qm[:, h, tk], kp[:, h // 2, tk], start=True, stop=True)
                last.then_inc(sem("qkb_ps"), 1)
                for q in range(2):
                    last = turn(bank(6, R, q, P), kp[:, q, tk], ident[:])
                last.then_inc(sem("kb_ps"), 1)
                pe.wait_ge(sem("mt"), t + 1)
                mm(PB[7][0:R, 0:H], lastr[:] if t < 2 else lastr_s[:], ms[0:R, t, MT, :], start=True, stop=True)\
                    .then_inc(sem("mnew_ps"), 1)
                pe.wait_ge(sem("s"), t + 1)
                for h in range(H):
                    last = turn(bank(5, R, h, R), M_S[0:R, h, 0:R], ident[0:R, 0:R])
                last.then_inc(sem("sT_ps"), 1)
                pe.wait_ge(sem("sT"), t + 1)
                for h in range(H):
                    last = mm(PB[1 + h // 2][0:R, 129 * (h % 2):129 * (h % 2) + 129], M_ST[0:R, h, 0:R], va[0:R, t, h, :],
                              start=True, stop=True)
                last.then_inc(sem("num_ps"), 1)
                if t == 1:
                    for h in range(H):
                        last = mm(PB[3 + h // 2][0:R, 129 * (h % 2):129 * (h % 2) + 129], qm[:, h, tk], Cp[:, h // 2, :],
                                  start=True, stop=True)
                    last.then_inc(sem("qC_ps"), 1)
                if t == 2:
                    pe.wait_ge(sem("C_in"), 16 * 4 * NSEQ)
                    for h in range(H):
                        for s in range(NSEQ):
                            c = 64 * h + LS * s
                            mm(PB[3][:, c:c + LS], Cs[:, s, h // 2, 0:DK], qm[:, h, o0 + LS * s:o0 + LS * s + LS],
                               start=True, stop=True)
                    for h in range(H):
                        last = mm(PB[3][0:R, 256 + NSEQ * h:256 + NSEQ * h + NSEQ], qm[:, h, tk], Cs[:, :, h // 2, DK],
                                  start=True, stop=True)
                    last.then_inc(sem("qCT_ps"), 1)
                    pe.wait_ge(sem("qCT"), 1)
                    for h in range(H):
                        last = turn(bank(4, R, h, P), stage[:, 64 * h:64 * h + 64], ident[:])
                    last.then_inc(sem("qC_ps"), 1)
                    pe.wait_ge(sem("fx"), 1)
                    mm(PB[7][:, 0:NSEQ * H], ones[0:64, :], fx[:].rearrange("p s h -> p (s h)"), start=True, stop=True)\
                        .then_inc(sem("ft_ps"), 1)
                pe.wait_ge(sem("kw"), t + 1)
                if t < 2:
                    for q in range(2):
                        for hh in range(2):
                            h = 2 * q + hh
                            last = mm(PB[6][:, 129 * q:129 * q + 129], M_KW[0:R, h, :], va[0:R, t, h, :],
                                      start=(hh == 0), stop=(hh == 1))
                    last.then_inc(sem("dC_ps"), 1)
                else:
                    for q in range(2):
                        pe.wait_ge(sem("vx"), H + q + 1)
                        if q > 0:
                            pe.wait_ge(sem("Cs_done"), q)
                        for n, (s0, s1) in enumerate([(0, 3), (3, 6), (6, 8)]):
                            for hh in range(2):
                                last = mm(PB[[5, 6, 0][n]][:, 0:129 * (s1 - s0)], M_KW[0:R, 2 * q + hh, :],
                                          vexp[hh][0:R, s0:s1, :], start=(hh == 0), stop=(hh == 1))
                        last.then_inc(sem("dC_ps"), 1)
                pe.wait_ge(sem("hn"), t + 1)
                for h in range(H):
                    last = turn(bank(3, P, h, R), B_O[0:R, h, :], ident[0:R, 0:R])
                last.then_inc(sem("mixT_ps"), 1)
            pe.wait_ge(sem("mix"), 6)
            pe.wait_ge(sem("wo_in"), 16)
            for i in range(6):
                t, n = i // 2, i % 2
                R = ROWS[t]
                if i >= 4:
                    pe.wait_ge(sem("x1"), i - 3)
                for k in range(KD):
                    last = mm(PB[i % 4][0:R, :], xT[:, k, OFF[t]:OFF[t] + R], wo[:, k, 512 * n:512 * n + 512],
                              start=(k == 0), stop=(k == KD - 1))
                last.then_inc(sem("x1_ps"), 1)
            turn_x(1, 4)
            pe.wait_ge(sem("xT"), 12)
            pe.wait_ge(sem("x1"), 6)
            pe.wait_ge(sem("rw_in"), 32)
            for t in range(3):
                R = ROWS[t]
                for k in range(KD):
                    last = mm(PB[0][0:R, NE * t:NE * t + NE], xT[:, k, OFF[t]:OFF[t] + R], rw[:, k, :],
                              start=(k == 0), stop=(k == KD - 1))
            last.then_inc(sem("lg_ps"), 1)
            pe.wait_ge(sem("member"), 1)
            for t in range(3):
                R = ROWS[t]
                for u in range(t + 1):
                    last = mm(PB[1][0:R, NE * t:NE * t + NE], (before if u == t else ones)[0:ROWS[u], 0:R], t3[0][0:ROWS[u], u, :],
                              start=(u == 0), stop=(u == t))
            for u in range(3):
                last = mm(PB[1][:, 96:96 + NE], ones[0:ROWS[u], :], t3[0][0:ROWS[u], u, :], start=(u == 0), stop=(u == 2))
            last.then_inc(sem("pos_ps"), 1)

            def gather(b):
                pe.wait_ge(sem("sel"), b + 1)
                for k in range(KD):
                    for t in range(3):
                        R = ROWS[t]
                        last = mm(PB[0][:, SL * k:SL * k + SL], XS[0:R, t, P * k:P * k + P], SEL[0:R, t, :],
                                  start=(k == 0 and t == 0), stop=(t == 2), skip_group_check=True)
                last.then_inc(sem("xg_ps"), 1)

            pe.wait_ge(sem("tables"), 1)
            total = pe.value_load(ntot[0:1, 0:1], min_val=NE, max_val=NB - 1)
            gather(0)
            with pe.Fori(0, total) as b:
                pe.wait_ge(sem("xg"), b + 1)
                for k in range(KD):
                    pe.wait_ge(sem(f"w_full{k}"), 16 * b + 16)
                    for m in range(16):
                        last = mm(PB[1 + m // 8][:, SL * (m % 8):SL * (m % 8) + SL], slot(k)[:, P * m:P * m + P], xg[:, k, :],
                                  start=(k == 0 and m % 8 == 0), stop=(k == KD - 1), skip_group_check=True)
                    last.then_inc(sem("w_used"), 1)
                gather(b + 1)
                pe.wait_ge(sem("selg"), b + 1)
                for t in range(3):
                    out, src, one = PB[6][0:SL, OFF[t]:OFF[t] + ROWS[t]], SELG[0:ROWS[t], t, :], ident[0:ROWS[t], 0:ROWS[t]]
                    last = mm(out, src, one, start=True, stop=True) if t == 0 else turn(out, src, one)
                last.then_inc(sem("selT_ps"), 1)
                pe.wait_ge(sem("act"), b + 1)
                for c in range(NDN):
                    pe.wait_ge(sem(f"w_full{NGU + c}"), 16 * b + 16)
                    for kk in range(2):
                        k = 2 * c + kk
                        for m in range(KD):
                            last = mm(PB[3][:, SL * m:SL * m + SL], slot(NGU + c)[:, D * kk + P * m:D * kk + P * m + P], act_t[:, k, :],
                                      start=(k == 0 and m == 0), stop=(k == KD - 1), skip_group_check=True)
                    last.then_inc(sem("w_used"), 1)
                pe.wait_ge(sem("ye"), b + 1)
                for m in range(KD):
                    out = PB[4 + m // 4][0:SL, P * (m % 4):P * (m % 4) + P]
                    last = mm(out, ye[:, m, :], ident[:], start=True, stop=True) if m == 0 else turn(out, ye[:, m, :], ident[:])
                last.then_inc(sem("yT_ps"), 1)
                pe.wait_ge(sem("yT"), b + 1)
                for i in range(6):
                    t, n = i // 2, i % 2
                    R = ROWS[t]
                    if i >= 2:
                        pe.wait_ge(sem("x2"), 6 * b + i - 1)
                    mm(PB[6 + n][:, :], SELT[0:SL, OFF[t]:OFF[t] + P], yT[0:SL, 512 * n:512 * n + 512],
                       start=True, stop=True).then_inc(sem("x2_ps"), 1)
                pe.wait_ge(sem("x2"), 6 * b + 6)
            nc.tensor.nop().then_inc(sem("moe_done"), 1)
            pe.wait_ge(sem("p_in"), 48)
            pe.wait_ge(sem("plw_in"), 16)
            for t in range(3):
                R = ROWS[t]
                for k in range(2):
                    last = turn(PB[k][:, OFF[t]:OFF[t] + R], ptk[0:R, t, P * k:P * k + P], ident[0:R, 0:R])
            last.then_inc(sem("pT_ps"), 1)
            pe.wait_ge(sem("pT"), 1)
            for i in range(6):
                t, n = i // 2, i % 2
                R = ROWS[t]
                if i >= 2:
                    pe.wait_ge(sem("pw"), i - 1)
                for k in range(2):
                    last = mm(PB[2 + i % 2][0:R, :], pT[:, k, OFF[t]:OFF[t] + R], plw[:, k, 512 * n:512 * n + 512],
                              start=(k == 0), stop=(k == 1))
                last.then_inc(sem("pw_ps"), 1)
            turn_x(2, 4)
            pe.wait_ge(sem("xT"), 18)
            pe.wait_ge(sem("wple_in"), 16)
            for i in range(6):
                t, n = i // 2, i % 2
                R = ROWS[t]
                if i >= 2:
                    pe.wait_ge(sem("gate"), i - 1)
                for k in range(KD):
                    last = mm(PB[6 + i % 2][0:R, :], xT[:, k, OFF[t]:OFF[t] + R], wple[:, k, 512 * n:512 * n + 512],
                              start=(k == 0), stop=(k == KD - 1))
                last.then_inc(sem("gate_ps"), 1)

        @block.scalar
        def _(act):
            A = nc.scalar.activation
            n = [0]

            def link(ins):
                n[0] += 1
                ins.then_inc(sem("act_chain"), 1)
                act.wait_ge(sem("act_chain"), n[0])

            def squares(t, scratch):
                R = ROWS[t]
                return A(scratch[0:R, :], X[0:R, t, :], ACT.Square, accum_out=nst[0:R, 0, t:t + 1])

            act.wait_ge(sem("consts1"), 1)
            act.wait_ge(sem("x_in"), 48)
            for t in range(3):
                last = squares(t, XS[:, t, :])
                last.then_inc(sem("ss"), 1)
            act.wait_ge(sem("pcolT"), 1)
            A(pcol[:, :], PB[0][:, 0:77], ACT.Copy).then_inc(sem("pcol"), 1)
            act.wait_ge(sem("rows_used"), 1)
            for w in range(CW - 1):
                last = A(xc[:, :, XCW + w::XCS], PB[1][:, 0:24 * NCH].rearrange("p (c s w) -> p c s w", c=NCH, w=CW - 1)[:, :, :, w],
                         ACT.Copy)
            last.then_inc(sem("rows_out"), 1)
            A(bgu[:].rearrange("p c e -> p (c e)"), PB[2][:, :], ACT.Copy).then_inc(sem("rows_out"), 1)
            A(bdn[:].rearrange("p c e -> p (c e)"), PB[3][:, 0:KD * NE], ACT.Copy).then_inc(sem("rows_out"), 1)
            act.wait_ge(sem("bc_in"), 64)
            act.wait_ge(sem("zabs"), 1)
            link(A(z8[:].rearrange("p t g -> p (t g)"), t8[:].rearrange("p t g -> p (t g)"), ACT.Exp, scale=-1.0))
            A(beta[:], g16[:, :, 4:8], ACT.Exp, scale=-1.0).then_inc(sem("expg"), 1)
            A(coef[:, 0:4], bc16[:, 0:4], ACT.Exp).then_inc(sem("expg"), 1)
            A(z8[:].rearrange("p t g -> p (t g)"), z8[:].rearrange("p t g -> p (t g)"), ACT.Ln, bias=ones[:, 0:1])\
                .then_inc(sem("expg"), 1)

            def seqs(ap, c):
                return ap

            def proj_out(j):
                g, c = PROD[j]
                name = GROUPS[g][0]
                act.wait_ge(sem("proj"), j + 1)
                src = PB[4 + j % 4]
                if name in ("k", "q", "v"):
                    ch = {"q": 0, "k": 4, "v": 8}[name] + c
                    A(xc[:, ch, CW - 1:XCW], src[:, 0:TP], ACT.Copy)
                    last = A(xc[:, ch, XCW:XC].rearrange("p (s x) -> p s x", s=NSEQ)[:, :, CW - 1:XCS],
                             src[:, TP:NTOK].rearrange("p (s x) -> p s x", s=NSEQ), ACT.Copy)
                elif name == "qkb" and c < 2:
                    A(qm[0:64, 2 * c, :], src[0:64, 0:NTOK], ACT.Copy, scale=DQ ** -0.5)
                    last = A(qm[64:128, 2 * c + 1, :], src[64:128, 0:NTOK], ACT.Copy, scale=DQ ** -0.5)
                elif name == "qkb":
                    last = A(kp[:, c - 2, :], src[:, 0:NTOK], ACT.Copy)
                elif name == "vb":
                    R = ROWS[c]
                    last = A(va[0:R, c, :, 0:DK], src[0:R, :].rearrange("p (h v) -> p h v", h=H), ACT.Copy)
                elif name == "z":
                    act.wait_ge(sem("proj"), j + 1)
                    last = A(szo[:, c, :], src[:, 0:NTOK], ACT.Silu)
                else:
                    last = A(szo[:, 4 + c, :], src[:, 0:NTOK], ACT.Sigmoid)
                if name in ("z", "ob"):
                    last.then_inc(sem("szo"), 1)
                    act.wait_ge(sem("szo"), (c if name == "z" else 4 + c) + 1)
                    nc.scalar.nop().then_inc(sem("proj_out"), 1)
                else:
                    last.then_inc(sem("proj_out"), 1)

            def silu(i):
                ch = (4 + i) if i < 4 else (i - 4 if i < 8 else i)
                act.wait_ge(sem("conv"), i + 1)
                src = scf[:, 512 * (i % 2):512 * (i % 2) + XC]
                A(qkv[:, ch, 0:TP], src[:, 0:TP], ACT.Silu)
                A(qkv[:, ch, TP:NTOK].rearrange("p (s x) -> p s x", s=NSEQ),
                  src[:, XCW:XC].rearrange("p (s x) -> p s x", s=NSEQ)[:, :, 0:LS], ACT.Silu).then_inc(sem("silu"), 1)

            for j in range(len(PROD)):
                proj_out(j)
                if 1 <= j <= 12:
                    silu(j - 1)
            for i in range(8):
                act.wait_ge(sem("nrm"), i + 1)
                if i >= 2:
                    act.wait_ge(sem("qkn"), i - 1)
                q = i >= 4
                A(SC[:, 2 + i % 2, 0:NTOK], PB[1 + i % 2][:, 0:NTOK], ACT.Sqrt, bias=epsc[:, 1:2] if q else epsc[:, 0:1],
                  scale=float(DK) if q else 1.0).then_inc(sem("nrm_out"), 1)
            for c in range(NCH):
                act.wait_ge(sem("cnewT"), c + 1)
                if c == 0:
                    act.wait_ge(sem("silu"), NCH)
                    act.wait_ge(sem("conv"), NCH)
                if c % 4 == 3:
                    A(crow[0:27, P * (c - 3):P * (c + 1)], PB[4][0:27, :], ACT.Copy).then_inc(sem("crow"), 4)
            act.wait_ge(sem("exarg"), 1)
            A(ex[:].rearrange("p t g -> p (t g)"), ex[:].rearrange("p t g -> p (t g)"), ACT.Exp).then_inc(sem("expx"), 1)
            act.wait_ge(sem("cum"), 1)
            A(egx[:].rearrange("p s g -> p (s g)"), PB[0][:, 64:128], ACT.Exp).then_inc(sem("expx"), 1)
            for t in range(3):
                R = ROWS[t]
                act.wait_ge(sem("edarg"), t + 1)
                A(B_ED[0:R, :, 0:R], B_ED[0:R, :, 0:R], ACT.Exp).then_inc(sem("ed"), 1)
                act.wait_ge(sem("marg"), t + 1)
                A(ms[0:R, t, EINT:EMT + 1, :], ms[0:R, t, EINT:EMT + 1, :], ACT.Exp).then_inc(sem("mexp"), 1)
                A(M_P[0:R, :, 0:R], M_P[0:R, :, 0:R], ACT.Exp).then_inc(sem("pexp"), 1)
                act.wait_ge(sem("warg"), t + 1)
                A(ms[0:R, t, WL:FT + 1, :], ms[0:R, t, WL:FT + 1, :], ACT.Exp).then_inc(sem("wexp"), 1)
            for t in range(3):
                act.wait_ge(sem("x1"), 2 * t + 2)
                if t == 0:
                    act.wait_ge(sem("xs_free"), 1)
                squares(t, XS[:, t, :]).then_inc(sem("ss"), 1)
            act.wait_ge(sem("larg"), 1)
            A(t3[1][:, :, :], t3[1][:, :, :], ACT.Exp).then_inc(sem("lexp"), 1)
            act.wait_ge(sem("tables"), 1)
            total = act.value_load(ntot[0:1, 0:1], min_val=NE, max_val=NB - 1)
            with act.Fori(0, total) as b:
                act.wait_ge(sem("selT_ps"), b + 1)
                A(SELT[0:SL, 0:NTOK], PB[6][0:SL, 0:NTOK], ACT.Copy).then_inc(sem("selT"), 1)
                act.wait_ge(sem("gt"), b + 1)
                A(sg, gt, ACT.Sigmoid, scale=ALPHA).then_inc(sem("sig"), 1)
                act.wait_ge(sem("yT_ps"), b + 1)
                A(yT[0:SL, 0:512], PB[4][0:SL, :], ACT.Copy)
                link_last = A(yT[0:SL, 512:1024], PB[5][0:SL, :], ACT.Copy)
                link_last.then_inc(sem("yT"), 1)
            act.wait_ge(sem("moe_done"), 1)
            for t in range(3):
                squares(t, XS[:, t, :]).then_inc(sem("ss"), 1)
            act.wait_ge(sem("pT_ps"), 1)
            for k in range(2):
                last = A(pT[:, k, :], PB[k][:, 0:NTOK], ACT.Copy)
            last.then_inc(sem("pT"), 1)
            for i in range(6):
                t, m = i // 2, i % 2
                act.wait_ge(sem("pw_ps"), i + 1)
                A(pw[0:ROWS[t], t, 512 * m:512 * m + 512], PB[2 + i % 2][0:ROWS[t], :], ACT.Copy).then_inc(sem("pw"), 1)
            for i in range(6):
                t, m = i // 2, i % 2
                act.wait_ge(sem("gate_ps"), i + 1)
                if i >= 2:
                    act.wait_ge(sem("x3"), i - 1)
                A(gsc[i % 2][0:ROWS[t], :], PB[6 + i % 2][0:ROWS[t], :], ACT.Sigmoid).then_inc(sem("gate"), 1)
                if m == 1:
                    act.wait_ge(sem("x3"), i + 1)
                    squares(t, XS[:, t, :]).then_inc(sem("ss"), 1)

        @block.vector
        def _(dve):
            V = nc.vector
            n = [0]

            def link(ins):
                n[0] += 1
                ins.then_inc(sem("dve_chain"), 1)
                dve.wait_ge(sem("dve_chain"), n[0])

            def tell(ins, name, by=1):
                ins.then_inc(sem(name), by)

            def norm(nth):
                dve.wait_ge(sem("ss"), 3 * nth + 3)
                tell(V.tensor_scalar(nst[:, 1, :], nst[:, 0, :], 1.0 / D, EPS, ALU.mult, ALU.add), "ms")
                dve.wait_ge(sem("rs"), nth + 1)
                for t in range(3):
                    R = ROWS[t]
                    tell(V.tensor_scalar(XS[0:R, t, :], X[0:R, t, :], nst[0:R, 2, t:t + 1], None, ALU.mult), "xs")

            def xT_out(nth, gain, b0):
                for i in range(6):
                    t, hb = i // 2, i % 2
                    R = ROWS[t]
                    dve.wait_ge(sem("xsT"), 6 * nth + i + 1)
                    src = PB[b0 + i % 2][:, :].rearrange("p (k x) -> p k x", k=4)[:, :, 0:R]
                    tell(V.tensor_tensor(xT[:, 4 * hb:4 * hb + 4, OFF[t]:OFF[t] + R], src,
                                         bc(pcol[:, gain + 4 * hb:gain + 4 * hb + 4], 2, R), ALU.mult), "xT")

            norm(0)
            dve.wait_ge(sem("pcol"), 1)
            xT_out(0, 0, 4)
            dve.wait_ge(sem("g16_ps"), 1)
            dve.wait_ge(sem("bc_in"), 64)
            V.tensor_copy(g16[:, 0:2, :].rearrange("p t g -> p (t g)"), PB[0][:, 0:32])
            link(V.tensor_copy(g16[0:64, 2, :], PB[0][0:64, 32:48]))
            V.tensor_tensor(gl8[:, :, 0:4], g16[:, :, 0:4], bc(bc16[:, 4:8], 1, 3), ALU.add)
            V.tensor_tensor(igc[:, :, :], g16[:, :, 8:12], bc(bc16[:, 8:12], 1, 3), ALU.add)
            link(V.scalar_tensor_tensor(gl8[:, :, 4:8], g16[:, :, 12:16], -1.0, bc(bc16[:, 12:16], 1, 3), ALU.mult, ALU.subtract))
            tell(V.scalar_tensor_tensor(t8[:, :, :], gl8[:, :, :], -1.0, gl8[:, :, :], ALU.mult, ALU.max), "zabs")
            dve.wait_ge(sem("expg"), 3)
            link(V.scalar_tensor_tensor(gl8[:, :, :], gl8[:, :, :], 0.0, z8[:, :, :], ALU.max, ALU.add))
            V.tensor_scalar(coef[:, 0:4], coef[:, 0:4], -1.0, None, ALU.mult)
            link(V.memset(coef[:, 4:8], -1.0))
            link(V.tensor_tensor(gl8[:, :, :], gl8[:, :, :], bc(coef[:, :], 1, 3), ALU.mult))
            link(V.tensor_scalar(beta[:, :, :], beta[:, :, :], 1.0, None, ALU.add))
            link(V.reciprocal(beta[:, :, :], beta[:, :, :]))
            dve.wait_ge(sem("consts2"), 1)
            tell(V.tensor_tensor(glx[:, :, :], bc(gl8[0:64, 2, :], 1, NSEQ), bc(inds[:, :], 2, 8), ALU.mult), "gl8")
            dve.wait_ge(sem("rows_out"), 1)
            L = XC - (CW - 1)
            for i in range(12):
                ch = (4 + i) if i < 4 else (i - 4 if i < 8 else i)
                dve.wait_ge(sem("proj_out"), i + 1)
                if i >= 2:
                    dve.wait_ge(sem("silu"), i - 1)
                acc = scf[:, 512 * (i % 2):512 * (i % 2) + L]
                for w in range(CW):
                    tap = pcol[:, 24 + 12 * w + ch:25 + 12 * w + ch]
                    if w == 0:
                        ins = V.tensor_scalar(acc, xc[:, ch, 0:L], tap, None, ALU.mult)
                    else:
                        ins = V.scalar_tensor_tensor(acc, xc[:, ch, w:w + L], tap, acc, ALU.mult, ALU.add)
                    if w < CW - 1:
                        link(ins)
                tell(ins, "conv")
            new = SC[:, 14, 0:27 * NCH].rearrange("p (c r) -> p c r", c=NCH)
            V.tensor_copy(new[:, :, 0:3], xc[:, :, TP:TP + 3])
            tell(V.tensor_copy(new[:, :, 3:27].rearrange("p c (s w) -> p c s w", w=3),
                               xc[:, :, XCW:XC].rearrange("p c (s x) -> p c s x", s=NSEQ)[:, :, :, LS:XCS]), "cnew")
            for i in range(8):
                ch = 4 + i if i < 4 else i - 4
                dve.wait_ge(sem("nrm_out"), i + 1)
                r = SC[:, 2 + i % 2, 0:NTOK]
                link(V.reciprocal(r, r))
                tell(V.tensor_tensor(qkv[:, ch, :], qkv[:, ch, :], r, ALU.mult), "qkn")
            dve.wait_ge(sem("cum"), 1)
            for dst, c in ((gcb, 0), (gto, 32)):
                V.tensor_copy(dst[:, 0:2, :].rearrange("p t g -> p (t g)"), PB[0][:, c:c + 16])
                last = V.tensor_copy(dst[0:64, 2, :], PB[0][0:64, c + 16:c + 24])
            link(last)
            V.tensor_copy(ex[:, :, 0:4], gcb[:, :, 0:4])
            V.tensor_tensor(ex[:, :, 4:8], gto[:, :, 0:4], gcb[:, :, 0:4], ALU.subtract)
            V.tensor_tensor(igc[:, :, :], igc[:, :, :], gcb[:, :, 4:8], ALU.subtract)
            tell(V.tensor_copy(ex[:, :, 8:12], gto[:, :, 0:4]), "exarg")
            dve.wait_ge(sem("expx"), 2)
            link(V.tensor_tensor(kco[:, :, :], beta[:, :, :], ex[:, :, 0:4], ALU.mult))
            V.nop().then_inc(sem("cum_out"), 1)
            dve.wait_ge(sem("qkn"), 8)

            levels = 0
            for t in range(3):
                R, o0 = ROWS[t], OFF[t]
                tk = slice(o0, o0 + R)
                nU, nL = (negU[:], negL[:]) if t < 2 else (negU_s[:], negL_s[:])

                def ps(b, w, R=R):
                    return PB[b][0:R, :].rearrange("p (h x) -> p h x", h=H)[:, :, 0:w]

                tell(V.tensor_tensor(B_DG[0:R, :, 0:R], bc(ident[0:R, 0:R], 1, H), bc(gcb[0:R, t, 0:4], 2, R), ALU.mult), "diag")
                dve.wait_ge(sem("R_ps"), t + 1)
                Rps = PB[0][0:R, 0:4 * R].rearrange("p (h x) -> p h x", h=H)
                link(V.tensor_tensor(B_ED[0:R, :, 0:R], Rps, bc(gcb[0:R, t, 0:4], 2, R), ALU.subtract))
                tell(V.tensor_tensor(B_ED[0:R, :, 0:R], B_ED[0:R, :, 0:R], bc(nU, 1, H), ALU.add), "edarg")
                dve.wait_ge(sem("kqv_ps"), 4 * t + 3)
                V.tensor_tensor(B_KBG[0:R, :, :], ps(3, P), bc(kco[0:R, t, :], 2, P), ALU.mult)
                V.tensor_tensor(B_KD[0:R, :, :], ps(3, P), bc(ex[0:R, t, 4:8], 2, P), ALU.mult)
                dve.wait_ge(sem("kqv_ps"), 4 * t + 4)
                V.tensor_tensor(B_VB[0:R, :, :], ps(4, P), bc(beta[0:R, t, :], 2, P), ALU.mult)
                dve.wait_ge(sem("ed"), t + 1)
                dve.wait_ge(sem("kqv_ps"), 4 * t + 1)
                link(V.tensor_tensor(B_P1[0:R, :, 0:R], ps(1, R), B_ED[0:R, :, 0:R], ALU.mult))
                tell(V.tensor_tensor(B_P1[0:R, :, 0:R], B_P1[0:R, :, 0:R], bc(before[0:R, 0:R], 1, H), ALU.mult), "P1")
                dve.wait_ge(sem("kqv_ps"), 4 * t + 2)
                V.tensor_tensor(B_QK[0:R, :, 0:R], ps(2, R), B_ED[0:R, :, 0:R], ALU.mult)
                dve.wait_ge(sem("A_ps"), t + 1)
                tell(V.tensor_tensor(B_A[0:R, :, 0:R], ps(5, R), bc(beta[0:R, t, :], 2, R), ALU.mult), "A")
                for l in range(7 if t < 2 else 3):
                    levels += 1
                    dve.wait_ge(sem("Y_ps"), levels)
                    tell(V.tensor_tensor(B_Y[0:R, :, 0:R], ps(5, R), bc(lvl[0:R, l, 0:R], 1, H), ALU.mult), "Y")
                    dve.wait_ge(sem("TW_ps"), levels)
                    old = [bc(ident[0:R, 0:R], 1, H)] * 2 if l == 0 else [B_T[0:R, :, 0:R], B_W[0:R, :, 0:R]]
                    V.tensor_tensor(B_T[0:R, :, 0:R], old[0], ps(6, R), ALU.subtract)
                    tell(V.tensor_tensor(B_W[0:R, :, 0:R], old[1], ps(7, R), ALU.subtract), "TW")
                dve.wait_ge(sem("u_ps"), t + 1)
                if t == 0:
                    tell(V.tensor_copy(B_VN[0:R, :, :], ps(5, P)), "vnew")
                else:
                    link(V.tensor_copy(B_VN[0:R, :, :], ps(5, P)))
                    dve.wait_ge(sem("wT_ps"), t)
                    tell(V.tensor_copy(B_WT[:, :, 0:R], PB[6][:, :].rearrange("p (h x) -> p h x", h=H)[:, :, 0:R]), "wT")
                    if t == 2:
                        dve.wait_ge(sem("wqST_ps"), 1)
                        tell(V.tensor_copy(stage, PB[7][:, :]), "wqST")
                    dve.wait_ge(sem("wqS_ps"), t)
                    tell(V.tensor_tensor(B_VN[0:R, :, :], B_VN[0:R, :, :], ps(7, P), ALU.subtract), "vnew")
                    link(V.tensor_tensor(B_O[0:R, :, :], ps(6, P), bc(ex[0:R, t, 0:4], 2, P), ALU.mult))
                dve.wait_ge(sem("o_ps"), t + 1)
                if t == 0:
                    link(V.tensor_copy(B_O[0:R, :, :], ps(1, P)))
                else:
                    link(V.tensor_tensor(B_O[0:R, :, :], B_O[0:R, :, :], ps(1, P), ALU.add))
                if t == 0:
                    dve.wait_ge(sem("dS_ps"), 1)
                    tell(V.tensor_copy(Sp, ps(2, P, P)), "Sp_done")
                elif t == 1:
                    link(V.tensor_tensor(Sp, Sp, bc(ex[:, 1, 8:12], 2, DK), ALU.mult))
                    dve.wait_ge(sem("dS_ps"), 2)
                    tell(V.tensor_tensor(Sp, Sp, ps(2, P, P), ALU.add), "Sp_done")
                else:
                    for h in range(H):
                        if h >= 2:
                            dve.wait_ge(sem("dS_ps"), 2 + h - 1)
                        tell(V.tensor_tensor(vexp[h % 2][:, :, 0:DK], bc(B_VN[0:R, h, :], 1, NSEQ), bc(inds[:, :], 2, DK), ALU.mult), "vx")
                        link(V.tensor_tensor(S[:, :, h, :], S[:, :, h, :], bc(egx[:, :, h], 2, DK), ALU.mult))
                        dve.wait_ge(sem("dS_ps"), 2 + h + 1)
                        V.tensor_tensor(S[:, 0:4, h, :], S[:, 0:4, h, :], ps(2, P, P), ALU.add)
                        tell(V.tensor_tensor(S[:, 4:8, h, :], S[:, 4:8, h, :], ps(3, P, P), ALU.add), "Ss_done")

                def head_norm(src, scratch, out, i):
                    link(V.tensor_tensor(scratch[0:R, :, :], src, src, ALU.mult))
                    link(V.tensor_reduce(st[0:R, t, i, :], scratch[0:R, :, :], AX, ALU.add))
                    tell(V.tensor_scalar(st[0:R, t, i, :], st[0:R, t, i, :], 1.0 / DK, EPS, ALU.mult, ALU.add), "hms")
                    dve.wait_ge(sem("hrs"), 2 * t + i + 1)
                    return V.tensor_tensor(out[0:R, :, :], src, bc(ms[0:R, t, 10 + i, :], 2, DK), ALU.mult)

                tell(head_norm(B_O[0:R, :, :], B_ED, B_DG, 0), "on")
                dve.wait_ge(sem("mixT_ps"), 2 * t + 1)
                if t == 0:
                    dve.wait_ge(sem("szg"), 8)
                    dve.wait_ge(sem("proj"), len(PROD))
                tell(V.tensor_tensor(xT[:, 0:4, tk], ps(0, R, P), szo[:, 0:4, tk], ALU.mult), "mix")
                m = lambda i: ms[0:R, t, i, :]
                tell(V.tensor_tensor(M_DG[0:R, :, 0:R], bc(ident[0:R, 0:R], 1, H), bc(igc[0:R, t, :], 2, R), ALU.mult), "diag")
                if t == 1:
                    V.tensor_copy(m(MPREV), ms[:, 0, MNEW, :])
                if t == 2:
                    dve.wait_ge(sem("m_in"), 16 * NSEQ)
                dve.wait_ge(sem("C_ps"), t + 1)
                Cps = PB[4][0:R, 0:4 * R].rearrange("p (h x) -> p h x", h=H)
                link(V.tensor_tensor(M_P[0:R, :, 0:R], Cps, bc(nL, 1, H), ALU.add))
                link(V.tensor_reduce(m(MCUM), M_P[0:R, :, 0:R], AX, ALU.max))
                link(V.tensor_tensor(m(MCUM), m(MCUM), m(MPREV), ALU.max))
                tell(V.tensor_tensor(m(MT), gcb[0:R, t, 4:8], m(MCUM), ALU.add), "mt")
                V.tensor_tensor(M_P[0:R, :, 0:R], M_P[0:R, :, 0:R], bc(m(MCUM), 2, R), ALU.subtract)
                link(V.tensor_tensor(m(EINT), m(MPREV), m(MCUM), ALU.subtract))
                dve.wait_ge(sem("mt"), t + 1)
                tell(V.tensor_scalar(m(EMT), m(MT), -1.0, None, ALU.mult), "marg")
                dve.wait_ge(sem("pexp"), t + 1)
                dve.wait_ge(sem("qkb_ps"), t + 1)
                tell(V.tensor_tensor(M_S[0:R, :, 0:R], ps(5, R), M_P[0:R, :, 0:R], ALU.mult), "s")
                dve.wait_ge(sem("mnew_ps"), t + 1)
                ins = V.tensor_copy(m(MNEW), PB[7][0:R, 0:H])
                tell(ins, "mnew")
                dve.wait_ge(sem("mnew"), t + 1)
                V.tensor_tensor(m(WL), igc[0:R, t, :], m(MNEW), ALU.subtract)
                link(V.tensor_tensor(m(FT), m(MPREV), m(MNEW), ALU.subtract))
                tell(V.tensor_tensor(ms[0:R, t, WL:FT + 1, :], ms[0:R, t, WL:FT + 1, :], bc(gto[0:R, t, 4:8], 1, 2), ALU.add), "warg")
                dve.wait_ge(sem("sT_ps"), t + 1)
                tell(V.tensor_copy(M_ST[0:R, :, 0:R], ps(5, R)), "sT")
                link(V.memset(M_KW[0:R, :, :], 0.0))
                dve.wait_ge(sem("wexp"), t + 1)
                dve.wait_ge(sem("kb_ps"), t + 1)
                for hh in range(2):
                    ins = V.tensor_tensor(M_KW[0:R, hh::2, 64 * hh:64 * hh + 64],
                                          PB[6][0:R, 0:256].rearrange("p (q x) -> p q x", q=2)[:, :, 64 * hh:64 * hh + 64],
                                          bc(ms[0:R, t, WL, hh::2], 2, DQ), ALU.mult)
                tell(ins, "kw")
                dve.wait_ge(sem("mexp"), t + 1)
                if t == 2:
                    dve.wait_ge(sem("qCT_ps"), 1)
                    V.tensor_tensor(qnx[:, :, :], PB[3][0:R, 256:288].rearrange("p (h s) -> p h s", h=H), bc(inds[:, :], 1, H), ALU.mult)
                    link(V.tensor_copy(stage[:, 0:256], PB[3][:, 0:256]))
                    tell(V.tensor_tensor(fx[:, :, :], bc(ms[0:R, t, FT, :], 1, NSEQ), bc(lasts[:, :], 2, H), ALU.mult), "fx")
                    dve.wait_ge(sem("fx"), 1)
                    V.nop().then_inc(sem("qCT"), 1)
                    link(V.tensor_reduce(M_NUM[0:R, :, DK], qnx[:, :, :], AX, ALU.add))
                    link(V.tensor_tensor(M_NUM[0:R, :, DK], M_NUM[0:R, :, DK], m(EINT), ALU.mult))
                dve.wait_ge(sem("num_ps"), t + 1)
                if t == 1:
                    dve.wait_ge(sem("qC_ps"), 1)
                if t == 2:
                    dve.wait_ge(sem("qC_ps"), 2)
                    link(V.tensor_tensor(M_NUM[0:R, :, 0:DK], ps(4, P), bc(m(EINT), 2, DK), ALU.mult))
                for q in range(2):
                    dst = M_NUM[0:R, 2 * q:2 * q + 2, :]
                    src = PB[1 + q][0:R, 0:258].rearrange("p (h v) -> p h v", h=2)
                    if t == 0:
                        ins = V.tensor_copy(dst, src)
                    else:
                        if t == 1:
                            link(V.tensor_tensor(dst, PB[3 + q][0:R, 0:258].rearrange("p (h v) -> p h v", h=2),
                                                 bc(ms[0:R, t, EINT, 2 * q:2 * q + 2], 2, DK + 1), ALU.mult))
                        ins = V.tensor_tensor(dst, dst, src, ALU.add)
                    link(ins)
                link(V.scalar_tensor_tensor(m(DEN), M_NUM[0:R, :, DK], -1.0, M_NUM[0:R, :, DK], ALU.mult, ALU.max))
                link(V.tensor_tensor(m(DEN), m(DEN), m(EMT), ALU.max))
                link(V.reciprocal(m(RDEN), m(DEN)))
                link(V.tensor_tensor(B_WT[0:R, :, :], M_NUM[0:R, :, 0:DK], bc(m(RDEN), 2, DK), ALU.mult))
                if t == 0:
                    dve.wait_ge(sem("dC_ps"), 1)
                    tell(V.tensor_copy(Cp, PB[6][:, 0:258].rearrange("p (q v) -> p q v", q=2)), "Cp_done")
                elif t == 1:
                    V.tensor_copy(ftp[0:64, 0, :], ms[0:64, 1, FT, 0::2])
                    link(V.tensor_copy(ftp[64:128, 0, :], ms[64:128, 1, FT, 1::2]))
                    link(V.tensor_tensor(Cp, Cp, bc(ftp[:, 0, :], 2, DK + 1), ALU.mult))
                    dve.wait_ge(sem("dC_ps"), 2)
                    tell(V.tensor_tensor(Cp, Cp, PB[6][:, 0:258].rearrange("p (q v) -> p q v", q=2), ALU.add), "Cp_done")
                else:
                    dve.wait_ge(sem("ft_ps"), 1)
                    for hh in range(2):
                        ins = V.tensor_copy(ftp[64 * hh:64 * hh + 64, :, :],
                                            PB[7][64 * hh:64 * hh + 64, 0:NSEQ * H].rearrange("p (s h) -> p s h", h=H)[:, :, hh::2])
                    link(ins)
                    for q in range(2):
                        if q > 0:
                            dve.wait_ge(sem("dC_ps"), 3)
                        for hh in range(2):
                            ins = V.tensor_tensor(vexp[hh][:, :, :], bc(va[0:R, 2, 2 * q + hh, :], 1, NSEQ), bc(inds[:, :], 2, DK + 1), ALU.mult)
                        tell(ins, "vx")
                        link(V.tensor_tensor(Cs[:, :, q, :], Cs[:, :, q, :], bc(ftp[:, :, q], 2, DK + 1), ALU.mult))
                        dve.wait_ge(sem("dC_ps"), 3 + q)
                        for nn, (s0, s1) in enumerate([(0, 3), (3, 6), (6, 8)]):
                            ins = V.tensor_tensor(Cs[:, s0:s1, q, :], Cs[:, s0:s1, q, :],
                                                  PB[[5, 6, 0][nn]][:, 0:129 * (s1 - s0)].rearrange("p (s v) -> p s v", v=129), ALU.add)
                        tell(ins, "Cs_done")
                tell(head_norm(B_WT[0:R, :, :], B_ED, B_O, 1), "hn")
                dve.wait_ge(sem("mixT_ps"), 2 * t + 2)
                tell(V.tensor_tensor(xT[:, 4:8, tk], ps(3, R, P), szo[:, 4:8, tk], ALU.mult), "mix")
            V.nop().then_inc(sem("xs_free"), 1)
            for i in range(6):
                t, m2 = i // 2, i % 2
                R = ROWS[t]
                dve.wait_ge(sem("x1_ps"), i + 1)
                dst = X[0:R, t, 512 * m2:512 * m2 + 512]
                tell(V.tensor_tensor(dst, dst, PB[i % 4][0:R, :], ALU.add), "x1")
            norm(1)
            xT_out(1, 8, 4)
            dve.wait_ge(sem("lg_ps"), 1)
            dve.wait_ge(sem("rw_in"), 32)
            V.tensor_tensor(lg[:, 0:2, :], PB[0][:, 0:64].rearrange("p (t e) -> p t e", t=2), bc(rbias[:, :], 1, 2), ALU.add)
            link(V.tensor_tensor(lg[0:64, 2, :], PB[0][0:64, 64:96], rbias[0:64, :], ALU.add))
            top = scf[:, 7424:7424 + 24].rearrange("p (t x) -> p t x", t=3)
            for t in range(3):
                ins = V.max(top[:, t, :], lg[:, t, :])
            link(ins)
            M_, E_, GT, EQ, INC, W1 = t3[0], t3[1], t3[2], t3[3], t3[4], t3[5]
            c4 = scf[:, 7460:7463]
            c5 = scf[:, 7464:7467]
            V.tensor_tensor(GT, lg[:], bc(top[:, :, 3], 2, NE), ALU.is_gt)
            V.tensor_tensor(EQ, lg[:], bc(top[:, :, 3], 2, NE), ALU.is_equal)
            tell(V.tensor_tensor(E_, lg[:], bc(top[:, :, 0], 2, NE), ALU.subtract), "larg")
            dve.wait_ge(sem("larg"), 1)
            for t in range(3):
                ins = V.tensor_tensor_scan(INC[:, t, :], ones[:, 0:NE], EQ[:, t, :], 0.0, ALU.mult, ALU.add)
            link(V.tensor_reduce(c4, GT, AX, ALU.add))
            link(V.tensor_scalar(c4, c4, -1.0, float(TOPK), ALU.mult, ALU.add))
            link(V.tensor_tensor(INC, INC, bc(c4, 2, NE), ALU.is_le))
            link(V.tensor_tensor(EQ, EQ, INC, ALU.mult))
            tell(V.tensor_tensor(M_, GT, EQ, ALU.add), "member")
            dve.wait_ge(sem("member"), 1)
            dve.wait_ge(sem("lexp"), 1)
            link(V.tensor_tensor(E_, E_, M_, ALU.mult))
            link(V.tensor_reduce(c5, E_, AX, ALU.add))
            link(V.reciprocal(c5, c5))
            link(V.tensor_tensor(gateb[:, :, 0:NE], E_, bc(c5, 2, NE), ALU.mult))
            dve.wait_ge(sem("pos_ps"), 1)
            link(V.scalar_tensor_tensor(posb[:, 0:2, 0:NE], PB[1][:, 0:64].rearrange("p (t e) -> p t e", t=2), 1.0, M_[:, 0:2, :],
                                        ALU.add, ALU.mult))
            link(V.scalar_tensor_tensor(posb[0:64, 2, 0:NE], PB[1][0:64, 64:96], 1.0, M_[0:64, 2, :], ALU.add, ALU.mult))
            link(V.memset(posb[64:128, 2, 0:NE], 0.0))
            link(V.tensor_scalar(posb[:, :, 0:NE], posb[:, :, 0:NE], -1.0, None, ALU.add))
            cnt, nov, cum, first = t1[0], t1[1], t1[2], t1[3]
            link(V.tensor_copy(cnt, PB[1][:, 96:96 + NE]))
            link(V.tensor_scalar(nov, cnt, float(SL), None, ALU.is_gt))
            for k in range(2, -(-NTOK // SL)):
                link(V.scalar_tensor_tensor(nov, cnt, float(SL * k), nov, ALU.is_gt, ALU.add))
            link(V.tensor_tensor_scan(cum, ones[:, 0:NE], nov, 0.0, ALU.mult, ALU.add))
            link(V.tensor_tensor(first, cum, nov, ALU.subtract))
            link(V.tensor_scalar(ntotf[:], cum[:, NE - 1:NE], float(NE), None, ALU.add))
            V.tensor_copy(ntot[:], ntotf[:])
            ej, fj, sj = scf[:, 7480:7480 + NOV], scf[:, 7510:7510 + NOV], scf[:, 7540:7540 + NOV]
            link(V.tensor_tensor(tb[0], bc(iota_s[:, 0:NOV], 2, NE), bc(cum, 1, NOV), ALU.is_ge))
            link(V.tensor_reduce(ej, tb[0], AX, ALU.add))
            link(V.tensor_tensor(tb[0], bc(iota_s[:, 0:NE], 1, NOV), bc(ej, 2, NE), ALU.is_equal))
            link(V.tensor_tensor(tb[1], tb[0], bc(first, 1, NOV), ALU.mult))
            link(V.tensor_reduce(fj, tb[1], AX, ALU.add))
            link(V.tensor_tensor(sj, iota_s[:, 0:NOV], fj, ALU.subtract))
            link(V.tensor_scalar(sj, sj, float(SL), float(SL), ALU.mult, ALU.add))
            for t in range(3):
                for src, dst in ((posb, posb), (gateb, gateb)):
                    link(V.tensor_tensor(tb[1], tb[0], bc(src[:, t, 0:NE], 1, NOV), ALU.mult))
                    link(V.tensor_reduce(dst[:, t, NE:NB], tb[1], AX, ALU.add))
                link(V.tensor_tensor(posb[:, t, NE:NB], posb[:, t, NE:NB], sj, ALU.subtract))
            V.memset(SELT[:, NTOK:3 * P], 0.0)
            V.tensor_copy(etabf[:, 0:NE], iota_s[:, 0:NE])
            link(V.tensor_scalar(etabf[:, NE:NB], ej, float(NE - 1), None, ALU.min))
            tell(V.tensor_copy(etab[:], etabf[:]), "tables")
            dve.wait_ge(sem("tables"), 1)

            def select(b):
                for t in range(3):
                    ins = V.tensor_scalar(SEL[:, t, :], iota_s[:], posb[:, t, bass.ds(b, 1)], None, ALU.is_equal)
                tell(ins, "sel")

            def gathered(b):
                dve.wait_ge(sem("xg_ps"), b + 1)
                tell(V.tensor_tensor(xg, PB[0][:, :].rearrange("p (k s) -> p k s", k=KD), bc(pcol[:, 8:16], 2, SL), ALU.mult), "xg")

            total = dve.value_load(ntot[0:1, 0:1], min_val=NE, max_val=NB - 1)
            select(0)
            gathered(0)
            with dve.Fori(0, total) as b:
                e = dve.value_load(etab[0:1, bass.ds(b, 1)], min_val=0, max_val=NE - 1)
                select(b + 1)
                for t in range(3):
                    ins = V.tensor_scalar(SELG[:, t, :], iota_s[:], posb[:, t, bass.ds(b, 1)], gateb[:, t, bass.ds(b, 1)],
                                          ALU.is_equal, ALU.mult)
                tell(ins, "selg")
                dve.wait_ge(sem("w_used"), NSLOT * b + NGU)
                bias = lambda c0: bgu[:, c0:c0 + 8, bass.ds(e, 1)].to_broadcast([P, 8, SL])
                V.tensor_tensor(gt, PB[1][:, :].rearrange("p (k s) -> p k s", k=KD), bias(0), ALU.add).then_inc(sem("lp"), 1)
                dve.wait_ge(sem("lp"), 4 * b + 1)
                V.tensor_scalar(gt, gt, LIMIT, None, ALU.min).then_inc(sem("gt"), 1)
                V.tensor_tensor(ut, PB[2][:, :].rearrange("p (k s) -> p k s", k=KD), bias(8), ALU.add).then_inc(sem("lp"), 1)
                dve.wait_ge(sem("lp"), 4 * b + 2)
                V.tensor_scalar(ut, ut, LIMIT, -LIMIT, ALU.min, ALU.max).then_inc(sem("lp"), 1)
                dve.wait_ge(sem("lp"), 4 * b + 3)
                dve.wait_ge(sem("gt"), b + 1)
                V.scalar_tensor_tensor(ut, ut, 1.0, gt, ALU.add, ALU.mult).then_inc(sem("lp"), 1)
                dve.wait_ge(sem("lp"), 4 * b + 4)
                dve.wait_ge(sem("sig"), b + 1)
                V.tensor_tensor(act_t, ut, sg, ALU.mult).then_inc(sem("act"), 1)
                gathered(b + 1)
                dve.wait_ge(sem("w_used"), NSLOT * b + NSLOT)
                V.tensor_tensor(ye, PB[3][:, :].rearrange("p (k s) -> p k s", k=KD),
                                bdn[:, :, bass.ds(e, 1)].to_broadcast([P, KD, SL]), ALU.add).then_inc(sem("ye"), 1)
                for i in range(6):
                    t, m2 = i // 2, i % 2
                    R = ROWS[t]
                    dve.wait_ge(sem("x2_ps"), 6 * b + i + 1)
                    dst = X[0:R, t, 512 * m2:512 * m2 + 512]
                    V.tensor_tensor(dst, dst, PB[6 + m2][0:R, :], ALU.add).then_inc(sem("x2"), 1)
            norm(2)
            xT_out(2, 16, 4)
            for i in range(6):
                t, m2 = i // 2, i % 2
                R = ROWS[t]
                dve.wait_ge(sem("gate"), i + 1)
                dve.wait_ge(sem("pw"), i + 1)
                link(V.tensor_tensor(gsc[i % 2][0:R, :], gsc[i % 2][0:R, :], pw[0:R, t, 512 * m2:512 * m2 + 512], ALU.mult))
                dst = X[0:R, t, 512 * m2:512 * m2 + 512]
                tell(V.tensor_tensor(dst, dst, gsc[i % 2][0:R, :], ALU.add), "x3")
                if m2 == 1:
                    dve.wait_ge(sem("ss"), 9 + t + 1)
                    tell(V.tensor_scalar(nst[0:R, 1, t:t + 1], nst[0:R, 0, t:t + 1], 1.0 / D, EPS, ALU.mult, ALU.add), "ms")
                    dve.wait_ge(sem("rs"), 3 + t + 1)
                    dve.wait_ge(sem("fg_in"), 16)
                    tell(V.scalar_tensor_tensor(X[0:R, t, :], X[0:R, t, :], nst[0:R, 2, t:t + 1], fgain[0:R, :],
                                                ALU.mult, ALU.mult), "y_ready")


_INS = ["x_prompt", "x_sample", "p_prompt", "p_sample", "state_conv", "state_gdn", "state_mlstm_c", "state_mlstm_n",
        "state_mlstm_m", "norm_attn_g", "w_in", "conv_w", "gdn_a_log", "gdn_dt_bias", "gdn_norm_g", "mlstm_i_bias",
        "mlstm_f_bias", "mlstm_norm_g", "w_out", "norm_moe_g", "router_w", "router_b", "expert_w_gu", "expert_b_gu",
        "expert_w_down", "expert_b_down", "norm_ple_g", "ple_gate_w", "ple_w", "final_norm_g"]
_OUTS = [("y_p", (1, TP, D)), ("y_s", (NSEQ, LS, D)), ("conv_p", (1, 1, CW - 1, NCH * P)), ("gdn_p", (1, 1, H, DK, DK)),
         ("c_p", (1, 1, H, DQ, DK)), ("n_p", (1, 1, H, DQ)), ("m_p", (1, 1, H)),
         ("conv_s", (1, NSEQ, CW - 1, NCH * P)), ("gdn_s", (1, NSEQ, H, DK, DK)), ("c_s", (1, NSEQ, H, DQ, DK)),
         ("n_s", (1, NSEQ, H, DQ)), ("m_s", (1, NSEQ, H))]


def kernel(**inputs):
    import numpy as _np
    import concourse.bacc as _bacc
    from concourse import mybir as _mybir
    from concourse.bass_utils import run_bass_kernel_spmd as _run

    nc = _bacc.Bacc("TRN2", target_bir_lowering=False, num_devices=1)
    arrays, a, o = {}, {}, {}
    for name in _INS:
        v = _np.ascontiguousarray(inputs[name])
        arrays[f"in_{name}"] = v
        a[name] = nc.dram_tensor(f"in_{name}", v.shape, _mybir.dt.from_np(v.dtype), kind="ExternalInput").ap()
    for name, shape in _OUTS:
        o[name] = nc.dram_tensor(f"out_{name}", shape, _mybir.dt.float32, kind="ExternalOutput").ap()
    build(nc, a, o)
    r = _run(nc, [arrays], core_ids=[0])
    return tuple(r.results[0][f"out_{name}"] for name, _ in _OUTS)
```

```python
from contextlib import ExitStack

import concourse.bass as bass
from concourse import mybir

F32 = mybir.dt.float32
I32 = mybir.dt.int32
F32R = mybir.dt.float32r
ALU = mybir.AluOpType
ACT = mybir.ActivationFunctionType
AX = mybir.AxisListType.X

P = 128
D = 1024
KD = D // P
FF = 1024
H = 4
DK = 128
DQ = 64
CW = 4
NCH = 12
NSEQ = 8
LS = 8
TP = 256
NTOK = TP + NSEQ * LS
ROWS = [128, 128, 64]
OFF = [0, 128, 256]
NE = 32
TOPK = 4
PLE = 256
EPS = 1e-6
NEG = -1e30
LIMIT = 7.0
ALPHA = 1.702
SL = 64
NOV = 24
NB = NE + NOV
SLOTW = 2048
NGU = 8
NDN = 4
NCK = NGU + NDN
NRAW = 6
NHI = 4
NSLOT = 12
XCW = CW - 1 + TP
XCS = CW - 1 + LS
XC = XCW + NSEQ * XCS
C_Z, C_AB, C_QB, C_VB, C_OB, C_IF = 1536, 2048, 2056, 2568, 3080, 3592


def bc(ap, axis, n):
    v = ap.unsqueeze(axis)
    shape = list(v.shape)
    shape[axis] = n
    return v.to_broadcast(shape)


def build(nc, a, o):
    with ExitStack() as ctx:
        sems = {}

        def sb(name, shape, dt=F32):
            return ctx.enter_context(nc.sbuf_tensor(name, shape, dt))

        def sem(name):
            if name not in sems:
                sems[name] = ctx.enter_context(nc.semaphore(name))
            return sems[name]

        def twin(name, shape):
            with nc.sbuf_tensor(name, shape, F32) as plain:
                pass
            return plain, sb(name + "_r", shape, F32R)

        ring, ring_r = twin("ring", [P, NSLOT * SLOTW])
        X = sb("X", [P, 3, D])
        XS, XH_r = twin("XS", [P, 3, D])
        xT = sb("xT", [P, KD, NTOK])
        szo = sb("szo", [P, 8, NTOK])
        qm = sb("qm", [P, H, NTOK])
        kp = sb("kp", [P, 2, NTOK])
        va = sb("va", [P, 3, H, DK + 1])
        SC, SC_r = twin("SC", [P, 15, H * P])
        ident = sb("ident", [P, P])
        ones = sb("ones", [P, P])
        upto = sb("upto", [P, P])
        upto_s = sb("upto_s", [64, 64])
        before = sb("before", [P, P])
        seg_s = sb("seg_s", [64, 64])
        negU = sb("negU", [P, P])
        negU_s = sb("negU_s", [64, 64])
        negL = sb("negL", [P, P])
        negL_s = sb("negL_s", [64, 64])
        lastr = sb("lastr", [P, P])
        lastr_s = sb("lastr_s", [64, 64])
        inds = sb("inds", [64, NSEQ])
        lasts = sb("lasts", [64, NSEQ])
        lvl = sb("lvl", [P, 7, P])
        iota_i = sb("iota_i", [P, SL], I32)
        iota_s = sb("iota_s", [P, SL])
        prow = sb("prow", [77, P])
        pcol = sb("pcol", [P, 77])
        bc16 = sb("bc16", [P, 16])
        rbias = sb("rbias", [P, NE])
        g16 = sb("g16", [P, 3, 16])
        z8 = sb("z8", [P, 3, 8])
        t8 = sb("t8", [P, 3, 8])
        gl8 = sb("gl8", [P, 3, 8])
        coef = sb("coef", [P, 8])
        beta = sb("beta", [P, 3, H])
        igc = sb("igc", [P, 3, H])
        gcb = sb("gcb", [P, 3, 8])
        gto = sb("gto", [P, 3, 8])
        ex = sb("ex", [P, 3, 12])
        kco = sb("kco", [P, 3, H])
        glx = sb("glx", [64, NSEQ, 8])
        egx = sb("egx", [P, NSEQ, 8])
        ms = sb("ms", [P, 3, 12, H])
        st = sb("st", [P, 3, 2, H])
        fx = sb("fx", [64, NSEQ, H])
        ftp = sb("ftp", [P, NSEQ, 2])
        qnx = sb("qnx", [64, H, NSEQ])
        nst = sb("nst", [P, 4, 3])
        mhalf = sb("mhalf", [P, 1])
        epsc = sb("epsc", [P, 2])
        bgu = sb("bgu", [P, 16, NE])
        w16 = sb("w16", [P, KD, 16])
        rw = sb("rw", [P, KD, NE])
        lg = sb("lg", [P, 3, NE])
        posb = sb("posb", [P, 3, NB])
        gateb = sb("gateb", [P, 3, NB])
        etabf = sb("etabf", [P, NB])
        etab = sb("etab", [P, NB], I32)
        ntotf = sb("ntotf", [P, 2])
        ntot = sb("ntot", [P, 2], I32)
        MPREV, MCUM, MT, MNEW, DEN, RDEN, EINT, EMT, WL, FT = range(10)

        PB = [ctx.enter_context(nc.psum_tensor(f"bank{i}", [P, 512], F32)) for i in range(8)]

        at = 0

        def take(n):
            nonlocal at
            at += n
            return ring[:, at - n:at]

        xcf = take(NCH * XC)
        xc = xcf.rearrange("p (c t) -> p c t", c=NCH)
        qkv = take(NCH * NTOK).rearrange("p (c t) -> p c t", c=NCH)
        S = take(NSEQ * H * DK).rearrange("p (s h v) -> p s h v", s=NSEQ, h=H)
        Cs = take(NSEQ * 2 * (DK + 1)).rearrange("p (s q v) -> p s q v", s=NSEQ, q=2)
        Sp = take(H * DK).rearrange("p (h v) -> p h v", h=H)
        Cp = take(2 * (DK + 1)).rearrange("p (q v) -> p q v", q=2)
        assert at <= NGU * SLOTW
        wbuf = [ring[:, (8 + 2 * i) * SLOTW:(10 + 2 * i) * SLOTW].rearrange("p (k n) -> p k n", k=KD) for i in range(2)]
        wo = ring[:, 8 * SLOTW:12 * SLOTW].rearrange("p (k n) -> p k n", k=KD)
        wple = ring[:, 0:4 * SLOTW].rearrange("p (k n) -> p k n", k=KD)
        fgain = ring[:, 4 * SLOTW:4 * SLOTW + D]
        srow = ring[:, 10 * SLOTW:11 * SLOTW]
        xs = XS[:, :, :].rearrange("p t d -> p (t d)")
        vexp = [xs[0:64, i * NSEQ * 129:(i + 1) * NSEQ * 129].rearrange("p (s v) -> p s v", s=NSEQ) for i in range(2)]
        crow = xcf[0:27, 0:NCH * P]
        scf = SC[:, :, :].rearrange("p b x -> p (b x)")

        def buf(i):
            return SC[:, i, :].rearrange("p (h x) -> p h x", h=H)

        B_DG, B_ED, B_P1, B_A, B_T, B_W, B_Y, B_QK, B_VB, B_KBG, B_KD, B_WT, B_VN, B_O, B_ST = (buf(i) for i in range(15))
        stage = SC[:, 14, :]
        M_DG, M_P, M_S, M_ST, M_KW = B_P1, B_A, B_T, B_W, B_Y
        M_NUM = scf[:, 8 * 512:8 * 512 + H * 129].rearrange("p (h v) -> p h v", h=H)

        e_at = 0

        def etake(n):
            nonlocal e_at
            e_at += n
            assert e_at <= 15 * 512
            return scf[:, e_at - n:e_at]

        scr = SC_r[:, :, :].rearrange("p b x -> p (b x)")
        etake(3 * SL)
        SEL_r = scr[:, e_at - 3 * SL:e_at].rearrange("p (t s) -> p t s", t=3)
        SELG = etake(3 * P).rearrange("p (t h s) -> p t h s", t=3, h=2)
        SELT = etake(NTOK)
        etake(KD * P)
        xg_r = scr[:, e_at - KD * P:e_at].rearrange("p (k s) -> p k s", k=KD)
        etake(KD * P)
        ag_r = scr[:, e_at - KD * P:e_at].rearrange("p (k h s) -> p k h s", k=KD, h=2)
        hS = etake(2 * FF)
        gt = etake(KD * SL).rearrange("p (k s) -> p k s", k=KD)
        ut = etake(KD * SL).rearrange("p (k s) -> p k s", k=KD)
        sg = etake(KD * SL).rearrange("p (k s) -> p k s", k=KD)
        act_t = etake(KD * SL).rearrange("p (k s) -> p k s", k=KD)
        gT = etake(NTOK)
        yS = qm[:, :, :].rearrange("p c t -> p (c t)")[:, 0:D]
        bdr = xT[:, :, :].rearrange("p c t -> p (c t)")[0:NE, 0:D]
        XL, XL_r = (x[:, 10 * SLOTW:10 * SLOTW + 3 * D].rearrange("p (t d) -> p t d", t=3) for x in (ring, ring_r))
        mgain = ring[:, 10 * SLOTW + 3 * D:10 * SLOTW + 4 * D]

        tb = [scf[:, 1024 * i:1024 * i + NOV * NE].rearrange("p (j e) -> p j e", j=NOV) for i in range(4)]
        t3 = [scf[:, 4096 + 128 * i:4096 + 128 * i + 3 * NE].rearrange("p (t e) -> p t e", t=3) for i in range(10)]
        t1 = [scf[:, 6144 + 64 * i:6144 + 64 * i + NE] for i in range(12)]
        pw = scf[:, 0:3 * D].rearrange("p (t d) -> p t d", t=3)
        gsc = [scf[:, 3 * D + 512 * i:3 * D + 512 * (i + 1)] for i in range(2)]
        szf = szo[:, :, :].rearrange("p c t -> p (c t)")
        plw = szf[:, 0:2048].rearrange("p (k n) -> p k n", k=2)
        qmf = qm[:, :, :].rearrange("p c t -> p (c t)")
        pT = qmf[:, 0:2 * NTOK].rearrange("p (k t) -> p k t", k=2)
        ptk = va[:, :, :, :].rearrange("p t h v -> p (t h v)")[:, 0:3 * PLE].rearrange("p (t d) -> p t d", t=3)

        x_in = [a["x_prompt"].rearrange("b t d -> (b t) d"), a["x_sample"].rearrange("b t d -> (b t) d")]
        p_in = [a["p_prompt"].rearrange("o b t d -> (o b t) d"), a["p_sample"].rearrange("o b t d -> (o b t) d")]
        y_out = [o["y_p"].rearrange("b t d -> (b t) d"), o["y_s"].rearrange("b t d -> (b t) d")]

        def tok_dram(pair, t):
            return pair[0][OFF[t]:OFF[t] + P, :] if t < 2 else pair[1]

        w_in = a["w_in"].rearrange("o (k p) n -> p (o k) n", p=P)
        w_out = a["w_out"].rearrange("o (k p) n -> p (o k) n", p=P)
        w_gu = a["expert_w_gu"].rearrange("o e (k p) n -> (o e) p k n", p=P)
        w_dn = a["expert_w_down"].rearrange("o e (k p) n -> (o e) p k n", p=P)

        def slot(c):
            return ring[:, c * SLOTW:(c + 1) * SLOTW]

        def raw(c):
            return slot(NHI + c % NRAW)

        def raw_r(c):
            return ring_r[:, (NHI + c % NRAW) * SLOTW:(NHI + c % NRAW + 1) * SLOTW]

        def hi_r(c):
            return ring_r[:, (c % NHI) * SLOTW:(c % NHI + 1) * SLOTW]

        def load_chunk(eng, e, c):
            if c < NGU:
                src, dst = w_gu[e, :, c, :], raw(c)
            else:
                k = 2 * (c - NGU)
                src, dst = w_dn[e, :, k:k + 2, :], raw(c).rearrange("p (k n) -> p k n", k=2)
            eng.dma_start(dst, src).then_inc(sem(f"w_full{c % NRAW}"), 16)

        POOL_LO = [2, 5, 8]

        def lo_count(b, c):
            mine = POOL_LO if c in POOL_LO else [x for x in range(NCK) if x not in POOL_LO]
            return sem("lo_pool" if c in POOL_LO else "lo_dve"), len(mine) * b + mine.index(c) + 1

        GROUPS = [("k", 512), ("q", 0), ("v", 1024), ("qkb", C_QB), ("vb", C_VB), ("z", C_Z), ("ob", C_OB)]
        NG = len(GROUPS)
        PROD = [(g, c) for g in range(NG) for c in range(3 if GROUPS[g][0] == "vb" else 4)]

        block = ctx.enter_context(nc.Block())

        @block.sync
        def _(sp):
            for t in range(3):
                sp.dma_start(X[0:ROWS[t], t, :], tok_dram(x_in, t)).then_inc(sem("x_in"), 16)
            rows = [("norm_attn_g", 0, 8), ("norm_moe_g", 8, 8), ("norm_ple_g", 16, 8), ("conv_w", 24, 48),
                    ("gdn_norm_g", 72, 1), ("mlstm_norm_g", 73, 4)]
            for name, r, n in rows:
                src = a[name].rearrange("o w (c p) -> (o w c) p", p=P) if name == "conv_w" else \
                    a[name].rearrange("o (c p) -> (o c) p", p=P)
                sp.dma_start(prow[r:r + n, :], src).then_inc(sem("params_in"), 16)
            for i, name in enumerate(["gdn_a_log", "gdn_dt_bias", "mlstm_i_bias", "mlstm_f_bias"]):
                sp.dma_start(bc16[:, 4 * i:4 * i + 4], a[name].to_broadcast([P, 4])).then_inc(sem("small_in"), 16)
            sp.dma_start(w16[:, :, 0:8], w_in[:, :, C_AB:C_AB + 8]).then_inc(sem("small_in"), 16)
            sp.dma_start(w16[:, :, 8:16], w_in[:, :, C_IF:C_IF + 8]).then_inc(sem("small_in"), 16)
            sp.dma_start(srow[0:24, 0:1536], a["state_conv"].rearrange("o b w c -> (o b w) c")).then_inc(sem("rows_in"), 16)
            sp.dma_start(srow[32:64, 0:2048], a["expert_b_gu"].rearrange("o e n -> (o e) n")).then_inc(sem("rows_in"), 16)
            for g, (_, c0) in enumerate(GROUPS):
                if g == 1:
                    sp.wait_ge(sem("rows_used"), 1)
                if g >= 2:
                    sp.wait_ge(sem("proj"), sum(x < g - 1 for x, _ in PROD))
                sp.dma_start(wbuf[g % 2], w_in[:, :, c0:c0 + 512]).then_inc(sem(f"group_in{g % 2}"), 16)
                if g == 1:
                    sp.wait_ge(sem("consts1"), 1)
                    for s in range(NSEQ):
                        sp.dma_start(S[:, s, :, :], a["state_gdn"][0, s].rearrange("h k v -> k h v")).then_inc(sem("S_in"), 16)
                        sp.dma_start(ms[LS * s:LS * s + LS, 2, MPREV, :], a["state_mlstm_m"][0, s:s + 1, :].to_broadcast([LS, H]))\
                            .then_inc(sem("S_in"), 16)
                        for q in range(2):
                            sp.dma_start(Cs[:, s, q, 0:DK], a["state_mlstm_c"][0, s, 2 * q:2 * q + 2].rearrange("h k v -> (h k) v"))\
                                .then_inc(sem("C_in"), 16)
                            sp.dma_start(Cs[:, s, q, DK:DK + 1], a["state_mlstm_n"][0, s, 2 * q:2 * q + 2, :]
                                         .rearrange("h (k u) -> (h k) u", u=1)).then_inc(sem("C_in"), 16)
                    sp.dma_start(rbias[:, :], a["router_b"].to_broadcast([P, NE])).then_inc(sem("rw_in"), 16)
                    sp.dma_start(rw[:, :, :], a["router_w"].rearrange("o (k p) n -> p (o k) n", p=P)).then_inc(sem("rw_in"), 16)
            sp.wait_ge(sem("proj"), len(PROD))
            sp.dma_start(wo, w_out).then_inc(sem("wo_in"), 16)
            nout = 0

            def store(dst, src):
                nonlocal nout
                nout += 1
                sp.dma_start(dst, src).then_inc(sem("out"), 16)

            sp.wait_ge(sem("crow"), NCH)
            store(o["conv_p"].rearrange("o b w c -> (o b w) c"), crow[0:3, :])
            store(o["conv_s"].rearrange("o b w c -> (o b w) c"), crow[3:27, :])
            sp.wait_ge(sem("Sp_done"), 2)
            store(o["gdn_p"][0, 0].rearrange("h k v -> k h v"), Sp)
            sp.wait_ge(sem("Cp_done"), 2)
            for q in range(2):
                store(o["c_p"][0, 0, 2 * q:2 * q + 2].rearrange("h k v -> (h k) v"), Cp[:, q, 0:DK])
                store(o["n_p"][0, 0, 2 * q:2 * q + 2].rearrange("h (k u) -> (h k) u", u=1), Cp[:, q, DK:DK + 1])
            sp.wait_ge(sem("mnew"), 3)
            store(o["m_p"][0], ms[0:1, 1, MNEW, :])
            for s in range(NSEQ):
                store(o["m_s"][0, s:s + 1, :], ms[LS * s:LS * s + 1, 2, MNEW, :])
            sp.wait_ge(sem("Ss_done"), H)
            sp.wait_ge(sem("Cs_done"), 2)
            for s in range(NSEQ):
                store(o["gdn_s"][0, s].rearrange("h k v -> k h v"), S[:, s, :, :])
                for q in range(2):
                    store(o["c_s"][0, s, 2 * q:2 * q + 2].rearrange("h k v -> (h k) v"), Cs[:, s, q, 0:DK])
                    store(o["n_s"][0, s, 2 * q:2 * q + 2].rearrange("h (k u) -> (h k) u", u=1), Cs[:, s, q, DK:DK + 1])
            sp.wait_ge(sem("out"), 16 * nout)
            sp.wait_ge(sem("x1"), 6)
            sp.nop().then_inc(sem("ring_free"), 1)
            sp.dma_start(mgain, a["norm_moe_g"].to_broadcast([P, D])).then_inc(sem("mgain_in"), 16)
            for c in range(NRAW):
                load_chunk(sp, 0, c)
            sp.dma_start(plw, a["ple_w"].rearrange("o (k p) n -> p (o k) n", p=P)).then_inc(sem("p_in"), 16)
            for t in range(3):
                sp.dma_start(ptk[0:ROWS[t], t, :], tok_dram(p_in, t)).then_inc(sem("p_in"), 16)
            sp.wait_ge(sem("lg_ps"), 1)
            sp.dma_start(bdr, a["expert_b_down"].rearrange("o e n -> (o e) n")).then_inc(sem("bdr_in"), 16)
            for c in range(NRAW, NCK):
                sp.wait_ge(sem("w_used"), c - NRAW + 1)
                load_chunk(sp, 0, c)
            sp.wait_ge(sem("tables"), 1)
            total = sp.value_load(ntot[0:1, 0:1], min_val=NE, max_val=NB - 1)
            with sp.Fori(1, total) as b:
                e = sp.value_load(etab[0:1, bass.ds(b, 1)], min_val=0, max_val=NE - 1)
                for c in range(NCK):
                    sp.wait_ge(sem("w_used"), NCK * b + (c - NRAW + 1))
                    load_chunk(sp, e, c)
            sp.wait_ge(sem("moe_done"), 1)
            sp.dma_start(wple, a["ple_gate_w"].rearrange("o (k p) n -> p (o k) n", p=P)).then_inc(sem("last_in"), 16)
            sp.dma_start(fgain, a["final_norm_g"].rearrange("(o d) -> o d", o=1).to_broadcast([P, D])).then_inc(sem("last_in"), 16)
            for t in range(3):
                sp.wait_ge(sem("y_ready"), t + 1)
                store(y_out[0][OFF[t]:OFF[t] + P, :] if t < 2 else y_out[1], X[0:ROWS[t], t, :])
            sp.wait_ge(sem("out"), 16 * nout)

        @block.gpsimd
        def _(pool):
            n = [0]

            def link(ins):
                n[0] += 1
                ins.then_inc(sem("pool_chain"), 1)
                pool.wait_ge(sem("pool_chain"), n[0])

            def keep(ap, pattern, base, cm, fill, op=ALU.is_ge):
                link(nc.gpsimd.affine_select(out=ap, in_=ap, compare_op=op, fill=fill, base=base, pattern=pattern,
                                             channel_multiplier=cm))

            def fill(ap, v):
                link(nc.gpsimd.memset(ap, v))

            fill(ident[:], 0.0)
            keep(ident[:], [[-1, P]], 0, 1, 1.0, ALU.not_equal)
            nc.gpsimd.memset(ones[:], 1.0).then_inc(sem("consts0"), 1)
            fill(epsc[:, 0:1], EPS)
            fill(epsc[:, 1:2], float(DK) * EPS)
            fill(mhalf[:], -0.5)
            fill(xc[:, :, 0:CW - 1], 0.0)
            fill(va[:, :, :, DK:DK + 1], 1.0)
            fill(qm[:], 0.0)
            fill(g16[:], 0.0)
            fill(gcb[:], 0.0)
            fill(gto[:], 0.0)
            fill(nst[:], 1.0)
            fill(lg[:], 0.0)
            nc.gpsimd.memset(ms[:], 0.0).then_inc(sem("consts1"), 1)

            def rsqrt(ready, count, done, out, in_):
                pool.wait_ge(sem(ready), count)
                sh = list(in_.shape)
                e = mhalf[0:sh[0], :] if len(sh) == 2 else None
                nc.gpsimd.tensor_tensor(out, in_, e.to_broadcast(sh), ALU.pow).then_inc(sem(done), 1)

            rsqrt("ms", 1, "rs", nst[:, 2, :], nst[:, 1, :])

            def segments(ap, cols=False):
                v = ap if cols else ap.rearrange("p (s i) -> p s i", s=NSEQ)
                z = [] if cols else [[0, LS]]
                keep(v, [[-LS, NSEQ]] + z, 0, 1, 0.0)
                keep(v, [[LS, NSEQ]] + z, LS - 1, -1, 0.0)

            fill(upto[:], 1.0)
            keep(upto[:], [[1, P]], 0, -1, 0.0)
            fill(seg_s[:], 1.0)
            segments(seg_s[:])
            fill(inds[:], 1.0)
            segments(inds[:], True)
            link(nc.gpsimd.tensor_tensor(upto_s[:], upto[0:64, 0:64], seg_s[:], ALU.mult))
            fill(before[:], 1.0)
            keep(before[:], [[1, P]], -1, -1, 0.0)
            fill(negU[:], 0.0)
            keep(negU[:], [[1, P]], 0, -1, NEG)
            link(nc.gpsimd.tensor_scalar(negU_s[:], upto_s[:], -1.0, -NEG, ALU.add, ALU.mult))
            fill(negL[:], 0.0)
            keep(negL[:], [[-1, P]], 0, 1, NEG)
            link(nc.gpsimd.tensor_scalar(negL_s[:], seg_s[:], -1.0, -NEG, ALU.add, ALU.mult))
            keep(negL_s[:], [[-1, 64]], 0, 1, NEG)
            fill(lastr[:], 1.0)
            keep(lastr[:], [[0, P]], -(P - 1), 1, 0.0)
            fill(lasts[:], 0.0)
            keep(lasts[:], [[-LS, NSEQ]], -(LS - 1), 1, 1.0, ALU.not_equal)
            fill(lastr_s[:], 0.0)
            keep(lastr_s[:].rearrange("p (s i) -> p s i", s=NSEQ), [[-LS, NSEQ], [0, LS]], -(LS - 1), 1, 1.0, ALU.not_equal)
            fill(lvl[:], 0.0)
            for l in range(7):
                s = 1 << l
                nb = P // (2 * s)
                v = lvl[:, l, :].rearrange("p (b x) -> p b x", b=nb)[:, :, s:2 * s]
                fill(v, 1.0)
                keep(v, [[-2 * s, nb], [0, s]], 0, 1, 0.0)
                keep(v, [[2 * s, nb], [0, s]], s - 1, -1, 0.0)
            link(nc.gpsimd.iota(iota_i[:], [[1, SL]], base=0, channel_multiplier=0))
            nc.gpsimd.tensor_copy(iota_s[:], iota_i[:]).then_inc(sem("consts2"), 1)
            order = [4, 5, 6, 7, 0, 1, 2, 3]
            pool.wait_ge(sem("xsT"), 6)
            for i, c in enumerate(order):
                pool.wait_ge(sem("silu"), i + 1)
                if i >= 2:
                    pool.wait_ge(sem("nrm"), i - 1)
                nc.gpsimd.tensor_tensor(XS[:, i % 2, 0:NTOK], qkv[:, c, :], qkv[:, c, :], ALU.mult).then_inc(sem("sq"), 1)
            for c in range(8):
                pool.wait_ge(sem("szo"), c + 1)
                gain = pcol[:, 72:73] if c < 4 else pcol[:, 69 + c:70 + c]
                nc.gpsimd.tensor_scalar(szo[:, c, :], szo[:, c, :], gain, None, ALU.mult).then_inc(sem("szg"), 1)
            for t in range(3):
                for i in range(2):
                    R = ROWS[t]
                    rsqrt("hms", 2 * t + i + 1, "hrs", ms[0:R, t, 10 + i, :], st[0:R, t, i, :])
            rsqrt("ms", 2, "rs", nst[:, 2, :], nst[:, 1, :])
            pool.wait_ge(sem("mgain_in"), 16)
            for t in range(3):
                R = ROWS[t]
                pool.wait_ge(sem("xs"), 3 + t + 1)
                nc.gpsimd.tensor_tensor(XL[0:R, t, :], XS[0:R, t, :], mgain[0:R, :], ALU.mult).then_inc(sem("xgain"), 1)
            for t in range(3):
                R = ROWS[t]
                pool.wait_ge(sem("XH"), t + 1)
                nc.gpsimd.tensor_tensor(XL_r[0:R, t, :], XL[0:R, t, :], XH_r[0:R, t, :], ALU.subtract).then_inc(sem("XL"), 1)

            def low(b, c):
                pool.wait_ge(sem("hi"), NCK * b + c + 1)
                nc.gpsimd.tensor_tensor(raw_r(c), raw(c), hi_r(c), ALU.subtract).then_inc(sem("lo_pool"), 1)

            pool.wait_ge(sem("tables"), 1)
            total = pool.value_load(ntot[0:1, 0:1], min_val=NE, max_val=NB - 1)
            for c in POOL_LO:
                low(0, c)
            with pool.Fori(1, total) as b:
                for c in POOL_LO:
                    low(b, c)
            rsqrt("ms", 3, "rs", nst[:, 2, :], nst[:, 1, :])
            for t in range(3):
                rsqrt("ms", 4 + t, "rs", nst[0:ROWS[t], 2, t:t + 1], nst[0:ROWS[t], 1, t:t + 1])

        @block.tensor
        def _(pe):
            mm = nc.tensor.matmul
            turn = nc.tensor.transpose

            def bank(b, R, h, w):
                return PB[b][0:R, h * P:h * P + w]

            pe.wait_ge(sem("consts0"), 1)
            pe.wait_ge(sem("params_in"), 16 * 6)
            turn(PB[0][:, 0:77], prow[:, :], ident[0:77, 0:77]).then_inc(sem("pcolT"), 1)
            pe.wait_ge(sem("rows_in"), 16 * 2)
            for c in range(NCH):
                turn(PB[1][:, 24 * c:24 * c + 24], srow[0:24, c * P:c * P + P], ident[0:24, 0:24])
            for c in range(16):
                last = turn(PB[2][:, NE * c:NE * c + NE], srow[32:64, c * P:c * P + P], ident[32:64, 32:64])
            last.then_inc(sem("rows_used"), 1)

            def turn_x(nth, b0):
                for t in range(3):
                    R = ROWS[t]
                    pe.wait_ge(sem("xs"), 3 * nth + t + 1)
                    for hb in range(2):
                        i = 2 * t + hb
                        if i >= 2:
                            pe.wait_ge(sem("xT"), 6 * nth + i - 1)
                        for k in range(4):
                            c = 4 * hb + k
                            last = turn(PB[b0 + i % 2][:, k * P:k * P + R], XS[0:R, t, c * P:c * P + P], ident[0:R, 0:R])
                        last.then_inc(sem("xsT"), 1)

            turn_x(0, 4)
            pe.wait_ge(sem("xT"), 6)
            pe.wait_ge(sem("small_in"), 96)
            pe.wait_ge(sem("pcol"), 1)
            for t in range(3):
                R = ROWS[t]
                for k in range(KD):
                    last = mm(PB[0][0:R, 16 * t:16 * t + 16], xT[:, k, OFF[t]:OFF[t] + R], w16[:, k, :],
                              start=(k == 0), stop=(k == KD - 1))
            last.then_inc(sem("g16_ps"), 1)
            for j, (g, c) in enumerate(PROD):
                if c == 0:
                    pe.wait_ge(sem(f"group_in{g % 2}"), 16 * (g // 2 + 1))
                if j >= 4:
                    pe.wait_ge(sem("proj_out"), j - 3)
                w = wbuf[g % 2]
                for k in range(KD):
                    if GROUPS[g][0] == "vb":
                        last = mm(PB[4 + j % 4][0:ROWS[c], :], xT[:, k, OFF[c]:OFF[c] + ROWS[c]], w[:, k, :],
                                  start=(k == 0), stop=(k == KD - 1))
                    else:
                        last = mm(PB[4 + j % 4][:, 0:NTOK], w[:, k, c * P:c * P + P], xT[:, k, :],
                                  start=(k == 0), stop=(k == KD - 1))
                last.then_inc(sem("proj"), 1)
            pe.wait_ge(sem("rows_out"), 2)
            for i in range(8):
                pe.wait_ge(sem("sq"), i + 1)
                if i >= 2:
                    pe.wait_ge(sem("nrm_out"), i - 1)
                mm(PB[1 + i % 2][:, 0:NTOK], ones[:], XS[:, i % 2, 0:NTOK], start=True, stop=True).then_inc(sem("nrm"), 1)
            pe.wait_ge(sem("cnew"), 1)
            pe.wait_ge(sem("proj_out"), len(PROD))
            for c in range(NCH):
                if c % 4 == 0:
                    if c:
                        pe.wait_ge(sem("crow"), c)
                turn(bank(4, 27, c % 4, P), SC[:, 14, 27 * c:27 * c + 27], ident[:]).then_inc(sem("cnewT"), 1)
            pe.wait_ge(sem("gl8"), 1)
            pe.wait_ge(sem("consts2"), 1)
            for t in range(3):
                R = ROWS[t]
                mm(PB[0][0:R, 8 * t:8 * t + 8], upto[:] if t < 2 else upto_s[:], gl8[0:R, t, :], start=True, stop=True)
                mm(PB[0][0:R, 32 + 8 * t:40 + 8 * t], ones[:] if t < 2 else seg_s[:], gl8[0:R, t, :], start=True, stop=True)
            mm(PB[0][:, 64:128], ones[0:64, :], glx[:].rearrange("p s g -> p (s g)"), start=True, stop=True)\
                .then_inc(sem("cum"), 1)
            pe.wait_ge(sem("cum_out"), 1)
            pe.wait_ge(sem("crow"), NCH)
            pe.wait_ge(sem("qkn"), 8)
            pe.wait_ge(sem("silu"), NCH)

            levels = 0
            for t in range(3):
                R, o0 = ROWS[t], OFF[t]
                tk = slice(o0, o0 + R)
                if t > 0:
                    pe.wait_ge(sem("mix"), 2 * t)
                pe.wait_ge(sem("diag"), 2 * t + 1)
                mm(PB[0][0:R, 0:4 * R], ones[0:R, 0:R], B_DG[0:R, :, 0:R], start=True, stop=True).then_inc(sem("R_ps"), 1)
                for h in range(H):
                    last = mm(bank(1, R, h, R), qkv[:, 4 + h, tk], qkv[:, 4 + h, tk], start=True, stop=True)
                last.then_inc(sem("kqv_ps"), 1)
                for h in range(H):
                    last = mm(bank(2, R, h, R), qkv[:, 4 + h, tk], qkv[:, h, tk], start=True, stop=True)
                last.then_inc(sem("kqv_ps"), 1)
                for h in range(H):
                    last = turn(bank(3, R, h, P), qkv[:, 4 + h, tk], ident[:])
                last.then_inc(sem("kqv_ps"), 1)
                for h in range(H):
                    last = turn(bank(4, R, h, P), qkv[:, 8 + h, tk], ident[:])
                last.then_inc(sem("kqv_ps"), 1)
                pe.wait_ge(sem("P1"), t + 1)
                for h in range(H):
                    last = turn(bank(5, R, h, R), B_P1[0:R, h, 0:R], ident[0:R, 0:R])
                last.then_inc(sem("A_ps"), 1)
                pe.wait_ge(sem("A"), t + 1)
                nl = 7 if t < 2 else 3
                for l in range(nl):
                    if l > 0:
                        pe.wait_ge(sem("TW"), levels)
                    levels += 1
                    Tl = [ident[0:R, 0:R] if l == 0 else B_T[0:R, h, 0:R] for h in range(H)]
                    Wl = [ident[0:R, 0:R] if l == 0 else B_W[0:R, h, 0:R] for h in range(H)]
                    for h in range(H):
                        last = mm(bank(5, R, h, R), B_A[0:R, h, 0:R], Wl[h], start=True, stop=True)
                    last.then_inc(sem("Y_ps"), 1)
                    pe.wait_ge(sem("Y"), levels)
                    for h in range(H):
                        mm(bank(6, R, h, R), B_Y[0:R, h, 0:R], Tl[h], start=True, stop=True)
                    for h in range(H):
                        last = mm(bank(7, R, h, R), Tl[h], B_Y[0:R, h, 0:R], start=True, stop=True)
                    last.then_inc(sem("TW_ps"), 1)
                pe.wait_ge(sem("TW"), levels)
                for h in range(H):
                    last = mm(bank(5, R, h, P), B_W[0:R, h, 0:R], B_VB[0:R, h, :], start=True, stop=True)
                last.then_inc(sem("u_ps"), 1)
                if t > 0:
                    for h in range(H):
                        last = mm(bank(6, P, h, R), B_KBG[0:R, h, :], B_W[0:R, h, 0:R], start=True, stop=True)
                    last.then_inc(sem("wT_ps"), 1)
                    pe.wait_ge(sem("wT"), t)
                if t == 1:
                    for h in range(H):
                        mm(bank(7, R, h, P), B_WT[:, h, 0:R], Sp[:, h, :], start=True, stop=True)
                    for h in range(H):
                        last = mm(bank(6, R, h, P), qkv[:, h, tk], Sp[:, h, :], start=True, stop=True)
                    last.then_inc(sem("wqS_ps"), 1)
                if t == 2:
                    pe.wait_ge(sem("S_in"), 32 * NSEQ)
                    for h in range(H):
                        for s in range(NSEQ):
                            c = 64 * h + LS * s
                            mm(PB[7][:, c:c + LS], S[:, s, h, :], B_WT[:, h, LS * s:LS * s + LS], start=True, stop=True)
                            last = mm(PB[7][:, 256 + c:256 + c + LS], S[:, s, h, :],
                                      qkv[:, h, o0 + LS * s:o0 + LS * s + LS], start=True, stop=True)
                    last.then_inc(sem("wqST_ps"), 1)
                    pe.wait_ge(sem("wqST"), 1)
                    for h in range(H):
                        turn(bank(7, R, h, P), stage[:, 64 * h:64 * h + 64], ident[:])
                    for h in range(H):
                        last = turn(bank(6, R, h, P), stage[:, 256 + 64 * h:256 + 64 * h + 64], ident[:])
                    last.then_inc(sem("wqS_ps"), 1)
                pe.wait_ge(sem("vnew"), t + 1)
                for h in range(H):
                    last = mm(bank(1, R, h, P), B_QK[0:R, h, 0:R], B_VN[0:R, h, :], start=True, stop=True)
                last.then_inc(sem("o_ps"), 1)
                if t < 2:
                    for h in range(H):
                        last = mm(bank(2, P, h, P), B_KD[0:R, h, :], B_VN[0:R, h, :], start=True, stop=True)
                    last.then_inc(sem("dS_ps"), 1)
                else:
                    for h in range(H):
                        pe.wait_ge(sem("vx"), h + 1)
                        if h > 0:
                            pe.wait_ge(sem("Ss_done"), h)
                        for n in range(2):
                            last = mm(PB[2 + n][:, :], B_KD[0:R, h, :], vexp[h % 2][0:R, 4 * n:4 * n + 4, 0:DK],
                                      start=True, stop=True)
                        last.then_inc(sem("dS_ps"), 1)
                pe.wait_ge(sem("on"), t + 1)
                for h in range(H):
                    last = turn(bank(0, P, h, R), B_DG[0:R, h, :], ident[0:R, 0:R])
                last.then_inc(sem("mixT_ps"), 1)
                pe.wait_ge(sem("diag"), 2 * t + 2)
                mm(PB[4][0:R, 0:4 * R], ones[0:R, 0:R], M_DG[0:R, :, 0:R], start=True, stop=True).then_inc(sem("C_ps"), 1)
                for h in range(H):
                    last = mm(bank(5, R, h, R), qm[:, h, tk], kp[:, h // 2, tk], start=True, stop=True)
                last.then_inc(sem("qkb_ps"), 1)
                for q in range(2):
                    last = turn(bank(6, R, q, P), kp[:, q, tk], ident[:])
                last.then_inc(sem("kb_ps"), 1)
                pe.wait_ge(sem("mt"), t + 1)
                mm(PB[7][0:R, 0:H], lastr[:] if t < 2 else lastr_s[:], ms[0:R, t, MT, :], start=True, stop=True)\
                    .then_inc(sem("mnew_ps"), 1)
                pe.wait_ge(sem("s"), t + 1)
                for h in range(H):
                    last = turn(bank(5, R, h, R), M_S[0:R, h, 0:R], ident[0:R, 0:R])
                last.then_inc(sem("sT_ps"), 1)
                pe.wait_ge(sem("sT"), t + 1)
                for h in range(H):
                    last = mm(PB[1 + h // 2][0:R, 129 * (h % 2):129 * (h % 2) + 129], M_ST[0:R, h, 0:R], va[0:R, t, h, :],
                              start=True, stop=True)
                last.then_inc(sem("num_ps"), 1)
                if t == 1:
                    for h in range(H):
                        last = mm(PB[3 + h // 2][0:R, 129 * (h % 2):129 * (h % 2) + 129], qm[:, h, tk], Cp[:, h // 2, :],
                                  start=True, stop=True)
                    last.then_inc(sem("qC_ps"), 1)
                if t == 2:
                    pe.wait_ge(sem("C_in"), 16 * 4 * NSEQ)
                    for h in range(H):
                        for s in range(NSEQ):
                            c = 64 * h + LS * s
                            mm(PB[3][:, c:c + LS], Cs[:, s, h // 2, 0:DK], qm[:, h, o0 + LS * s:o0 + LS * s + LS],
                               start=True, stop=True)
                    for h in range(H):
                        last = mm(PB[3][0:R, 256 + NSEQ * h:256 + NSEQ * h + NSEQ], qm[:, h, tk], Cs[:, :, h // 2, DK],
                                  start=True, stop=True)
                    last.then_inc(sem("qCT_ps"), 1)
                    pe.wait_ge(sem("qCT"), 1)
                    for h in range(H):
                        last = turn(bank(4, R, h, P), stage[:, 64 * h:64 * h + 64], ident[:])
                    last.then_inc(sem("qC_ps"), 1)
                    pe.wait_ge(sem("fx"), 1)
                    mm(PB[7][:, 0:NSEQ * H], ones[0:64, :], fx[:].rearrange("p s h -> p (s h)"), start=True, stop=True)\
                        .then_inc(sem("ft_ps"), 1)
                pe.wait_ge(sem("kw"), t + 1)
                if t < 2:
                    for q in range(2):
                        for hh in range(2):
                            h = 2 * q + hh
                            last = mm(PB[6][:, 129 * q:129 * q + 129], M_KW[0:R, h, :], va[0:R, t, h, :],
                                      start=(hh == 0), stop=(hh == 1))
                    last.then_inc(sem("dC_ps"), 1)
                else:
                    for q in range(2):
                        pe.wait_ge(sem("vx"), H + q + 1)
                        if q > 0:
                            pe.wait_ge(sem("Cs_done"), q)
                        for n, (s0, s1) in enumerate([(0, 3), (3, 6), (6, 8)]):
                            for hh in range(2):
                                last = mm(PB[[5, 6, 0][n]][:, 0:129 * (s1 - s0)], M_KW[0:R, 2 * q + hh, :],
                                          vexp[hh][0:R, s0:s1, :], start=(hh == 0), stop=(hh == 1))
                        last.then_inc(sem("dC_ps"), 1)
                pe.wait_ge(sem("hn"), t + 1)
                for h in range(H):
                    last = turn(bank(3, P, h, R), B_O[0:R, h, :], ident[0:R, 0:R])
                last.then_inc(sem("mixT_ps"), 1)
            pe.wait_ge(sem("mix"), 6)
            pe.wait_ge(sem("wo_in"), 16)
            for i in range(6):
                t, n = i // 2, i % 2
                R = ROWS[t]
                if i >= 4:
                    pe.wait_ge(sem("x1"), i - 3)
                for k in range(KD):
                    last = mm(PB[i % 4][0:R, :], xT[:, k, OFF[t]:OFF[t] + R], wo[:, k, 512 * n:512 * n + 512],
                              start=(k == 0), stop=(k == KD - 1))
                last.then_inc(sem("x1_ps"), 1)
            turn_x(1, 4)
            pe.wait_ge(sem("xT"), 12)
            pe.wait_ge(sem("x1"), 6)
            pe.wait_ge(sem("rw_in"), 32)
            for t in range(3):
                R = ROWS[t]
                for k in range(KD):
                    last = mm(PB[0][0:R, NE * t:NE * t + NE], xT[:, k, OFF[t]:OFF[t] + R], rw[:, k, :],
                              start=(k == 0), stop=(k == KD - 1))
            last.then_inc(sem("lg_ps"), 1)
            pe.wait_ge(sem("member"), 1)
            for t in range(3):
                R = ROWS[t]
                for u in range(t + 1):
                    last = mm(PB[1][0:R, NE * t:NE * t + NE], (before if u == t else ones)[0:ROWS[u], 0:R], t3[0][0:ROWS[u], u, :],
                              start=(u == 0), stop=(u == t))
            for u in range(3):
                last = mm(PB[1][:, 96:96 + NE], ones[0:ROWS[u], :], t3[0][0:ROWS[u], u, :], start=(u == 0), stop=(u == 2))
            last.then_inc(sem("pos_ps"), 1)

            pe.wait_ge(sem("gates"), 1)
            for t in range(3):
                last = turn(PB[2][0:NE, OFF[t]:OFF[t] + ROWS[t]], gateb[0:ROWS[t], t, 0:NE], ident[0:ROWS[t], 0:ROWS[t]])
            last.then_inc(sem("gT_ps"), 1)
            pe.wait_ge(sem("gT"), 1)
            pe.wait_ge(sem("bdr_in"), 16)
            for i in range(6):
                t, n = i // 2, i % 2
                if i >= 2:
                    pe.wait_ge(sem("x1"), 6 + i - 1)
                mm(PB[4 + n][0:ROWS[t], :], gT[0:NE, OFF[t]:OFF[t] + ROWS[t]], bdr[:, 512 * n:512 * n + 512],
                   start=True, stop=True).then_inc(sem("x1_ps"), 1)

            def gather(b, half):
                if half == 0:
                    pe.wait_ge(sem("sel"), b + 1)
                for k in range(4 * half, 4 * half + 4):
                    for part, src in enumerate((XH_r, XL_r)):
                        for t in range(3):
                            R = ROWS[t]
                            at0 = P * (k % 4) + SL * part
                            last = mm(PB[6 + half][:, at0:at0 + SL], src[0:R, t, P * k:P * k + P], SEL_r[0:R, t, :],
                                      start=(k % 4 == 0 and part == 0 and t == 0), stop=(t == 2), skip_group_check=True)
                last.then_inc(sem("xg_ps"), 1)

            def turn_select(b):
                pe.wait_ge(sem("xg"), 2 * b + 3)
                pe.wait_ge(sem("selg"), b + 1)
                for t in range(3):
                    R = ROWS[t]
                    last = mm(PB[6][:, OFF[t]:OFF[t] + R], SELG[0:R, t, :, :].rearrange("p h s -> p (h s)"), ident[0:R, 0:R],
                              start=True, stop=True)
                last.then_inc(sem("selT_ps"), 1)

            def scatter(b, i):
                t, n = i // 2, i % 2
                if i == 0:
                    pe.wait_ge(sem("selT"), b + 1)
                    pe.wait_ge(sem("yS"), 2 * b + 2)
                if i >= 2:
                    pe.wait_ge(sem("x2"), 6 * b + i - 1)
                mm(PB[4 + n][0:ROWS[t], :], SELT[:, OFF[t]:OFF[t] + ROWS[t]], yS[:, 512 * n:512 * n + 512],
                   start=True, stop=True).then_inc(sem("x2_ps"), 1)

            def chunk(b, c, last_c, lhs, out):
                s_, v = lo_count(b, c)
                pe.wait_ge(sem("hi"), NCK * b + c + 1)
                rows_ = 1 if c < NGU else 2
                width = SLOTW // rows_
                for kk in range(rows_):
                    for part, w in enumerate((hi_r(c), raw_r(c))):
                        if part == 1 and kk == 0:
                            pe.wait_ge(s_, v)
                        for n in range(width // 512):
                            first = (c in (0, NGU)) and kk == 0 and part == 0
                            last = mm(PB[out + n][:, :], lhs(rows_ * (c if c < NGU else c - NGU) + kk),
                                      w[:, width * kk + 512 * n:width * kk + 512 * n + 512],
                                      start=first, stop=(c == last_c and kk == rows_ - 1 and part == 1), skip_group_check=True)
                last.then_inc(sem("w_used"), 1)

            def expert(b, first):
                pe.wait_ge(sem("xg"), 2 * b + 2)
                for c in range(NGU):
                    chunk(b, c, NGU - 1, lambda k: xg_r[:, k, :], 0)
                    if c >= 2 and not first:
                        scatter(b - 1, c - 2)
                gather(b + 1, 0)
                pe.wait_ge(sem("hS"), 2 * b + 2)
                for m in range(2 * KD):
                    out, src = PB[m // 4][:, P * (m % 4):P * (m % 4) + P], hS[:, P * m:P * m + P]
                    last = turn(out, src, ident[:, :])
                    if m % 8 == 7:
                        last.then_inc(sem("hT_ps"), 1)
                gather(b + 1, 1)
                if not first:
                    pe.wait_ge(sem("x2"), 6 * b)
                pe.wait_ge(sem("act"), b + 1)
                for c in range(NGU, NCK):
                    chunk(b, c, NCK - 1, lambda k: ag_r[:, k, :, :].rearrange("p h s -> p (h s)"), 4)
                turn_select(b)

            pe.wait_ge(sem("XL"), 3)
            pe.wait_ge(sem("x1"), 12)
            pe.wait_ge(sem("tables"), 1)
            total = pe.value_load(ntot[0:1, 0:1], min_val=NE, max_val=NB - 1)
            gather(0, 0)
            gather(0, 1)
            expert(0, True)
            with pe.Fori(1, total) as b:
                expert(b, False)
            last_b = pe.value_load(ntot[0:1, 1:2], min_val=NE - 1, max_val=NB - 2)
            for i in range(6):
                scatter(last_b, i)
            pe.wait_ge(sem("x2"), 6 * total)
            nc.tensor.nop().then_inc(sem("moe_done"), 1)
            pe.wait_ge(sem("p_in"), 64)
            for t in range(3):
                R = ROWS[t]
                for k in range(2):
                    last = turn(PB[k][:, OFF[t]:OFF[t] + R], ptk[0:R, t, P * k:P * k + P], ident[0:R, 0:R])
            last.then_inc(sem("pT_ps"), 1)
            pe.wait_ge(sem("pT"), 1)
            for i in range(6):
                t, n = i // 2, i % 2
                R = ROWS[t]
                if i >= 2:
                    pe.wait_ge(sem("pw"), i - 1)
                for k in range(2):
                    last = mm(PB[2 + i % 2][0:R, :], pT[:, k, OFF[t]:OFF[t] + R], plw[:, k, 512 * n:512 * n + 512],
                              start=(k == 0), stop=(k == 1))
                last.then_inc(sem("pw_ps"), 1)
            turn_x(2, 4)
            pe.wait_ge(sem("xT"), 18)
            pe.wait_ge(sem("last_in"), 32)
            for i in range(6):
                t, n = i // 2, i % 2
                R = ROWS[t]
                if i >= 2:
                    pe.wait_ge(sem("gate"), i - 1)
                for k in range(KD):
                    last = mm(PB[6 + i % 2][0:R, :], xT[:, k, OFF[t]:OFF[t] + R], wple[:, k, 512 * n:512 * n + 512],
                              start=(k == 0), stop=(k == KD - 1))
                last.then_inc(sem("gate_ps"), 1)

        @block.scalar
        def _(act):
            A = nc.scalar.activation
            n = [0]

            def link(ins):
                n[0] += 1
                ins.then_inc(sem("act_chain"), 1)
                act.wait_ge(sem("act_chain"), n[0])

            def squares(t, scratch):
                R = ROWS[t]
                return A(scratch[0:R, :], X[0:R, t, :], ACT.Square, accum_out=nst[0:R, 0, t:t + 1])

            act.wait_ge(sem("consts1"), 1)
            act.wait_ge(sem("x_in"), 48)
            for t in range(3):
                last = squares(t, XS[:, t, :])
                last.then_inc(sem("ss"), 1)
            act.wait_ge(sem("pcolT"), 1)
            A(pcol[:, :], PB[0][:, 0:77], ACT.Copy).then_inc(sem("pcol"), 1)
            act.wait_ge(sem("rows_used"), 1)
            for w in range(CW - 1):
                last = A(xc[:, :, XCW + w::XCS], PB[1][:, 0:24 * NCH].rearrange("p (c s w) -> p c s w", c=NCH, w=CW - 1)[:, :, :, w],
                         ACT.Copy)
            last.then_inc(sem("rows_out"), 1)
            A(bgu[:].rearrange("p c e -> p (c e)"), PB[2][:, :], ACT.Copy).then_inc(sem("rows_out"), 1)
            act.wait_ge(sem("small_in"), 96)
            act.wait_ge(sem("zabs"), 1)
            link(A(z8[:].rearrange("p t g -> p (t g)"), t8[:].rearrange("p t g -> p (t g)"), ACT.Exp, scale=-1.0))
            A(beta[:], g16[:, :, 4:8], ACT.Exp, scale=-1.0).then_inc(sem("expg"), 1)
            A(coef[:, 0:4], bc16[:, 0:4], ACT.Exp).then_inc(sem("expg"), 1)
            A(z8[:].rearrange("p t g -> p (t g)"), z8[:].rearrange("p t g -> p (t g)"), ACT.Ln, bias=ones[:, 0:1])\
                .then_inc(sem("expg"), 1)

            def seqs(ap, c):
                return ap

            def proj_out(j):
                g, c = PROD[j]
                name = GROUPS[g][0]
                act.wait_ge(sem("proj"), j + 1)
                src = PB[4 + j % 4]
                if name in ("k", "q", "v"):
                    ch = {"q": 0, "k": 4, "v": 8}[name] + c
                    A(xc[:, ch, CW - 1:XCW], src[:, 0:TP], ACT.Copy)
                    last = A(xc[:, ch, XCW:XC].rearrange("p (s x) -> p s x", s=NSEQ)[:, :, CW - 1:XCS],
                             src[:, TP:NTOK].rearrange("p (s x) -> p s x", s=NSEQ), ACT.Copy)
                elif name == "qkb" and c < 2:
                    A(qm[0:64, 2 * c, :], src[0:64, 0:NTOK], ACT.Copy, scale=DQ ** -0.5)
                    last = A(qm[64:128, 2 * c + 1, :], src[64:128, 0:NTOK], ACT.Copy, scale=DQ ** -0.5)
                elif name == "qkb":
                    last = A(kp[:, c - 2, :], src[:, 0:NTOK], ACT.Copy)
                elif name == "vb":
                    R = ROWS[c]
                    last = A(va[0:R, c, :, 0:DK], src[0:R, :].rearrange("p (h v) -> p h v", h=H), ACT.Copy)
                elif name == "z":
                    act.wait_ge(sem("proj"), j + 1)
                    last = A(szo[:, c, :], src[:, 0:NTOK], ACT.Silu)
                else:
                    last = A(szo[:, 4 + c, :], src[:, 0:NTOK], ACT.Sigmoid)
                if name in ("z", "ob"):
                    last.then_inc(sem("szo"), 1)
                    act.wait_ge(sem("szo"), (c if name == "z" else 4 + c) + 1)
                    nc.scalar.nop().then_inc(sem("proj_out"), 1)
                else:
                    last.then_inc(sem("proj_out"), 1)

            def silu(i):
                ch = (4 + i) if i < 4 else (i - 4 if i < 8 else i)
                act.wait_ge(sem("conv"), i + 1)
                src = scf[:, 512 * (i % 2):512 * (i % 2) + XC]
                A(qkv[:, ch, 0:TP], src[:, 0:TP], ACT.Silu)
                A(qkv[:, ch, TP:NTOK].rearrange("p (s x) -> p s x", s=NSEQ),
                  src[:, XCW:XC].rearrange("p (s x) -> p s x", s=NSEQ)[:, :, 0:LS], ACT.Silu).then_inc(sem("silu"), 1)

            for j in range(len(PROD)):
                proj_out(j)
                if 1 <= j <= 12:
                    silu(j - 1)
            for i in range(8):
                act.wait_ge(sem("nrm"), i + 1)
                if i >= 2:
                    act.wait_ge(sem("qkn"), i - 1)
                q = i >= 4
                A(SC[:, 2 + i % 2, 0:NTOK], PB[1 + i % 2][:, 0:NTOK], ACT.Sqrt, bias=epsc[:, 1:2] if q else epsc[:, 0:1],
                  scale=float(DK) if q else 1.0).then_inc(sem("nrm_out"), 1)
            for c in range(NCH):
                act.wait_ge(sem("cnewT"), c + 1)
                if c == 0:
                    act.wait_ge(sem("silu"), NCH)
                    act.wait_ge(sem("conv"), NCH)
                if c % 4 == 3:
                    A(crow[0:27, P * (c - 3):P * (c + 1)], PB[4][0:27, :], ACT.Copy).then_inc(sem("crow"), 4)
            act.wait_ge(sem("exarg"), 1)
            A(ex[:].rearrange("p t g -> p (t g)"), ex[:].rearrange("p t g -> p (t g)"), ACT.Exp).then_inc(sem("expx"), 1)
            act.wait_ge(sem("cum"), 1)
            A(egx[:].rearrange("p s g -> p (s g)"), PB[0][:, 64:128], ACT.Exp).then_inc(sem("expx"), 1)
            for t in range(3):
                R = ROWS[t]
                act.wait_ge(sem("edarg"), t + 1)
                A(B_ED[0:R, :, 0:R], B_ED[0:R, :, 0:R], ACT.Exp).then_inc(sem("ed"), 1)
                act.wait_ge(sem("marg"), t + 1)
                A(ms[0:R, t, EINT:EMT + 1, :], ms[0:R, t, EINT:EMT + 1, :], ACT.Exp).then_inc(sem("mexp"), 1)
                A(M_P[0:R, :, 0:R], M_P[0:R, :, 0:R], ACT.Exp).then_inc(sem("pexp"), 1)
                act.wait_ge(sem("warg"), t + 1)
                A(ms[0:R, t, WL:FT + 1, :], ms[0:R, t, WL:FT + 1, :], ACT.Exp).then_inc(sem("wexp"), 1)
            for t in range(3):
                act.wait_ge(sem("x1"), 2 * t + 2)
                if t == 0:
                    act.wait_ge(sem("xs_free"), 1)
                squares(t, XS[:, t, :]).then_inc(sem("ss"), 1)
            act.wait_ge(sem("larg"), 1)
            A(t3[1][:, :, :], t3[1][:, :, :], ACT.Exp).then_inc(sem("lexp"), 1)
            for t in range(3):
                act.wait_ge(sem("xgain"), t + 1)
                act.wait_ge(sem("xsT"), 6 + 2 * t + 2)
                A(XH_r[0:ROWS[t], t, :], XL[0:ROWS[t], t, :], ACT.Copy).then_inc(sem("XH"), 1)
            act.wait_ge(sem("gT_ps"), 1)
            A(gT[0:NE, :], PB[2][0:NE, 0:NTOK], ACT.Copy).then_inc(sem("gT"), 1)

            def gathered(b, half):
                act.wait_ge(sem("xg_ps"), 2 * b + half + 1)
                A(xg_r[:, 4 * half:4 * half + 4, :].rearrange("p k s -> p (k s)"), PB[6 + half][:, :], ACT.Copy).then_inc(sem("xg"), 1)

            def high(b, c):
                act.wait_ge(sem(f"w_full{c % NRAW}"), 32 * b + 16 * (c // NRAW) + 16)
                if not (type(b) is int and b == 0 and c < NHI):
                    act.wait_ge(sem("w_used"), NCK * b + (c - NHI + 1))
                A(hi_r(c), raw(c), ACT.Copy).then_inc(sem("hi"), 1)

            def take_y(b):
                act.wait_ge(sem("w_used"), NCK * b + NCK)
                for n in range(2):
                    A(yS[:, 512 * n:512 * n + 512], PB[4 + n][:, :], ACT.Copy).then_inc(sem("yS"), 1)

            def take_select(b):
                act.wait_ge(sem("selT_ps"), b + 1)
                A(SELT, PB[6][:, 0:NTOK], ACT.Copy).then_inc(sem("selT"), 1)

            def expert(b, first):
                for c in range(NGU):
                    if c == 3 and not first:
                        take_select(b - 1)
                        take_y(b - 1)
                    high(b, c)
                act.wait_ge(sem("w_used"), NCK * b + NGU)
                A(hS[:, 0:512], PB[0][:, :], ACT.Copy)
                A(hS[:, 512:1024], PB[1][:, :], ACT.Copy).then_inc(sem("hS"), 1)
                gathered(b + 1, 0)
                high(b, 8)
                act.wait_ge(sem("gt"), b + 1)
                A(sg, gt, ACT.Sigmoid, scale=ALPHA).then_inc(sem("sig"), 1)
                high(b, 9)
                gathered(b + 1, 1)
                high(b, 10)
                high(b, 11)

            act.wait_ge(sem("ring_free"), 1)
            act.wait_ge(sem("tables"), 1)
            total = act.value_load(ntot[0:1, 0:1], min_val=NE, max_val=NB - 1)
            gathered(0, 0)
            gathered(0, 1)
            expert(0, True)
            with act.Fori(1, total) as b:
                expert(b, False)
            last_b = act.value_load(ntot[0:1, 1:2], min_val=NE - 1, max_val=NB - 2)
            take_select(last_b)
            take_y(last_b)
            act.wait_ge(sem("moe_done"), 1)
            for t in range(3):
                squares(t, XS[:, t, :]).then_inc(sem("ss"), 1)
            act.wait_ge(sem("pT_ps"), 1)
            for k in range(2):
                last = A(pT[:, k, :], PB[k][:, 0:NTOK], ACT.Copy)
            last.then_inc(sem("pT"), 1)
            for i in range(6):
                t, m = i // 2, i % 2
                act.wait_ge(sem("pw_ps"), i + 1)
                A(pw[0:ROWS[t], t, 512 * m:512 * m + 512], PB[2 + i % 2][0:ROWS[t], :], ACT.Copy).then_inc(sem("pw"), 1)
            for i in range(6):
                t, m = i // 2, i % 2
                act.wait_ge(sem("gate_ps"), i + 1)
                if i >= 2:
                    act.wait_ge(sem("x3"), i - 1)
                A(gsc[i % 2][0:ROWS[t], :], PB[6 + i % 2][0:ROWS[t], :], ACT.Sigmoid).then_inc(sem("gate"), 1)
                if m == 1:
                    act.wait_ge(sem("x3"), i + 1)
                    squares(t, XS[:, t, :]).then_inc(sem("ss"), 1)

        @block.vector
        def _(dve):
            V = nc.vector
            n = [0]

            def link(ins):
                n[0] += 1
                ins.then_inc(sem("dve_chain"), 1)
                dve.wait_ge(sem("dve_chain"), n[0])

            def tell(ins, name, by=1):
                ins.then_inc(sem(name), by)

            def norm(nth):
                dve.wait_ge(sem("ss"), 3 * nth + 3)
                tell(V.tensor_scalar(nst[:, 1, :], nst[:, 0, :], 1.0 / D, EPS, ALU.mult, ALU.add), "ms")
                dve.wait_ge(sem("rs"), nth + 1)
                for t in range(3):
                    R = ROWS[t]
                    tell(V.tensor_scalar(XS[0:R, t, :], X[0:R, t, :], nst[0:R, 2, t:t + 1], None, ALU.mult), "xs")

            def xT_out(nth, gain, b0):
                for i in range(6):
                    t, hb = i // 2, i % 2
                    R = ROWS[t]
                    dve.wait_ge(sem("xsT"), 6 * nth + i + 1)
                    src = PB[b0 + i % 2][:, :].rearrange("p (k x) -> p k x", k=4)[:, :, 0:R]
                    tell(V.tensor_tensor(xT[:, 4 * hb:4 * hb + 4, OFF[t]:OFF[t] + R], src,
                                         bc(pcol[:, gain + 4 * hb:gain + 4 * hb + 4], 2, R), ALU.mult), "xT")

            norm(0)
            dve.wait_ge(sem("pcol"), 1)
            xT_out(0, 0, 4)
            dve.wait_ge(sem("g16_ps"), 1)
            dve.wait_ge(sem("small_in"), 96)
            V.tensor_copy(g16[:, 0:2, :].rearrange("p t g -> p (t g)"), PB[0][:, 0:32])
            link(V.tensor_copy(g16[0:64, 2, :], PB[0][0:64, 32:48]))
            V.tensor_tensor(gl8[:, :, 0:4], g16[:, :, 0:4], bc(bc16[:, 4:8], 1, 3), ALU.add)
            V.tensor_tensor(igc[:, :, :], g16[:, :, 8:12], bc(bc16[:, 8:12], 1, 3), ALU.add)
            link(V.scalar_tensor_tensor(gl8[:, :, 4:8], g16[:, :, 12:16], -1.0, bc(bc16[:, 12:16], 1, 3), ALU.mult, ALU.subtract))
            tell(V.scalar_tensor_tensor(t8[:, :, :], gl8[:, :, :], -1.0, gl8[:, :, :], ALU.mult, ALU.max), "zabs")
            dve.wait_ge(sem("expg"), 3)
            link(V.scalar_tensor_tensor(gl8[:, :, :], gl8[:, :, :], 0.0, z8[:, :, :], ALU.max, ALU.add))
            V.tensor_scalar(coef[:, 0:4], coef[:, 0:4], -1.0, None, ALU.mult)
            link(V.memset(coef[:, 4:8], -1.0))
            link(V.tensor_tensor(gl8[:, :, :], gl8[:, :, :], bc(coef[:, :], 1, 3), ALU.mult))
            link(V.tensor_scalar(beta[:, :, :], beta[:, :, :], 1.0, None, ALU.add))
            link(V.reciprocal(beta[:, :, :], beta[:, :, :]))
            dve.wait_ge(sem("consts2"), 1)
            tell(V.tensor_tensor(glx[:, :, :], bc(gl8[0:64, 2, :], 1, NSEQ), bc(inds[:, :], 2, 8), ALU.mult), "gl8")
            dve.wait_ge(sem("rows_out"), 1)
            L = XC - (CW - 1)
            for i in range(12):
                ch = (4 + i) if i < 4 else (i - 4 if i < 8 else i)
                dve.wait_ge(sem("proj_out"), i + 1)
                if i >= 2:
                    dve.wait_ge(sem("silu"), i - 1)
                acc = scf[:, 512 * (i % 2):512 * (i % 2) + L]
                for w in range(CW):
                    tap = pcol[:, 24 + 12 * w + ch:25 + 12 * w + ch]
                    if w == 0:
                        ins = V.tensor_scalar(acc, xc[:, ch, 0:L], tap, None, ALU.mult)
                    else:
                        ins = V.scalar_tensor_tensor(acc, xc[:, ch, w:w + L], tap, acc, ALU.mult, ALU.add)
                    if w < CW - 1:
                        link(ins)
                tell(ins, "conv")
            new = SC[:, 14, 0:27 * NCH].rearrange("p (c r) -> p c r", c=NCH)
            V.tensor_copy(new[:, :, 0:3], xc[:, :, TP:TP + 3])
            tell(V.tensor_copy(new[:, :, 3:27].rearrange("p c (s w) -> p c s w", w=3),
                               xc[:, :, XCW:XC].rearrange("p c (s x) -> p c s x", s=NSEQ)[:, :, :, LS:XCS]), "cnew")
            for i in range(8):
                ch = 4 + i if i < 4 else i - 4
                dve.wait_ge(sem("nrm_out"), i + 1)
                r = SC[:, 2 + i % 2, 0:NTOK]
                link(V.reciprocal(r, r))
                tell(V.tensor_tensor(qkv[:, ch, :], qkv[:, ch, :], r, ALU.mult), "qkn")
            dve.wait_ge(sem("cum"), 1)
            for dst, c in ((gcb, 0), (gto, 32)):
                V.tensor_copy(dst[:, 0:2, :].rearrange("p t g -> p (t g)"), PB[0][:, c:c + 16])
                last = V.tensor_copy(dst[0:64, 2, :], PB[0][0:64, c + 16:c + 24])
            link(last)
            V.tensor_copy(ex[:, :, 0:4], gcb[:, :, 0:4])
            V.tensor_tensor(ex[:, :, 4:8], gto[:, :, 0:4], gcb[:, :, 0:4], ALU.subtract)
            V.tensor_tensor(igc[:, :, :], igc[:, :, :], gcb[:, :, 4:8], ALU.subtract)
            tell(V.tensor_copy(ex[:, :, 8:12], gto[:, :, 0:4]), "exarg")
            dve.wait_ge(sem("expx"), 2)
            link(V.tensor_tensor(kco[:, :, :], beta[:, :, :], ex[:, :, 0:4], ALU.mult))
            V.nop().then_inc(sem("cum_out"), 1)
            dve.wait_ge(sem("qkn"), 8)

            levels = 0
            for t in range(3):
                R, o0 = ROWS[t], OFF[t]
                tk = slice(o0, o0 + R)
                nU, nL = (negU[:], negL[:]) if t < 2 else (negU_s[:], negL_s[:])

                def ps(b, w, R=R):
                    return PB[b][0:R, :].rearrange("p (h x) -> p h x", h=H)[:, :, 0:w]

                tell(V.tensor_tensor(B_DG[0:R, :, 0:R], bc(ident[0:R, 0:R], 1, H), bc(gcb[0:R, t, 0:4], 2, R), ALU.mult), "diag")
                dve.wait_ge(sem("R_ps"), t + 1)
                Rps = PB[0][0:R, 0:4 * R].rearrange("p (h x) -> p h x", h=H)
                link(V.tensor_tensor(B_ED[0:R, :, 0:R], Rps, bc(gcb[0:R, t, 0:4], 2, R), ALU.subtract))
                tell(V.tensor_tensor(B_ED[0:R, :, 0:R], B_ED[0:R, :, 0:R], bc(nU, 1, H), ALU.add), "edarg")
                dve.wait_ge(sem("kqv_ps"), 4 * t + 3)
                V.tensor_tensor(B_KBG[0:R, :, :], ps(3, P), bc(kco[0:R, t, :], 2, P), ALU.mult)
                V.tensor_tensor(B_KD[0:R, :, :], ps(3, P), bc(ex[0:R, t, 4:8], 2, P), ALU.mult)
                dve.wait_ge(sem("kqv_ps"), 4 * t + 4)
                V.tensor_tensor(B_VB[0:R, :, :], ps(4, P), bc(beta[0:R, t, :], 2, P), ALU.mult)
                dve.wait_ge(sem("ed"), t + 1)
                dve.wait_ge(sem("kqv_ps"), 4 * t + 1)
                link(V.tensor_tensor(B_P1[0:R, :, 0:R], ps(1, R), B_ED[0:R, :, 0:R], ALU.mult))
                tell(V.tensor_tensor(B_P1[0:R, :, 0:R], B_P1[0:R, :, 0:R], bc(before[0:R, 0:R], 1, H), ALU.mult), "P1")
                dve.wait_ge(sem("kqv_ps"), 4 * t + 2)
                V.tensor_tensor(B_QK[0:R, :, 0:R], ps(2, R), B_ED[0:R, :, 0:R], ALU.mult)
                dve.wait_ge(sem("A_ps"), t + 1)
                tell(V.tensor_tensor(B_A[0:R, :, 0:R], ps(5, R), bc(beta[0:R, t, :], 2, R), ALU.mult), "A")
                for l in range(7 if t < 2 else 3):
                    levels += 1
                    dve.wait_ge(sem("Y_ps"), levels)
                    tell(V.tensor_tensor(B_Y[0:R, :, 0:R], ps(5, R), bc(lvl[0:R, l, 0:R], 1, H), ALU.mult), "Y")
                    dve.wait_ge(sem("TW_ps"), levels)
                    old = [bc(ident[0:R, 0:R], 1, H)] * 2 if l == 0 else [B_T[0:R, :, 0:R], B_W[0:R, :, 0:R]]
                    V.tensor_tensor(B_T[0:R, :, 0:R], old[0], ps(6, R), ALU.subtract)
                    tell(V.tensor_tensor(B_W[0:R, :, 0:R], old[1], ps(7, R), ALU.subtract), "TW")
                dve.wait_ge(sem("u_ps"), t + 1)
                if t == 0:
                    tell(V.tensor_copy(B_VN[0:R, :, :], ps(5, P)), "vnew")
                else:
                    link(V.tensor_copy(B_VN[0:R, :, :], ps(5, P)))
                    dve.wait_ge(sem("wT_ps"), t)
                    tell(V.tensor_copy(B_WT[:, :, 0:R], PB[6][:, :].rearrange("p (h x) -> p h x", h=H)[:, :, 0:R]), "wT")
                    if t == 2:
                        dve.wait_ge(sem("wqST_ps"), 1)
                        tell(V.tensor_copy(stage, PB[7][:, :]), "wqST")
                    dve.wait_ge(sem("wqS_ps"), t)
                    tell(V.tensor_tensor(B_VN[0:R, :, :], B_VN[0:R, :, :], ps(7, P), ALU.subtract), "vnew")
                    link(V.tensor_tensor(B_O[0:R, :, :], ps(6, P), bc(ex[0:R, t, 0:4], 2, P), ALU.mult))
                dve.wait_ge(sem("o_ps"), t + 1)
                if t == 0:
                    link(V.tensor_copy(B_O[0:R, :, :], ps(1, P)))
                else:
                    link(V.tensor_tensor(B_O[0:R, :, :], B_O[0:R, :, :], ps(1, P), ALU.add))
                if t == 0:
                    dve.wait_ge(sem("dS_ps"), 1)
                    tell(V.tensor_copy(Sp, ps(2, P, P)), "Sp_done")
                elif t == 1:
                    link(V.tensor_tensor(Sp, Sp, bc(ex[:, 1, 8:12], 2, DK), ALU.mult))
                    dve.wait_ge(sem("dS_ps"), 2)
                    tell(V.tensor_tensor(Sp, Sp, ps(2, P, P), ALU.add), "Sp_done")
                else:
                    for h in range(H):
                        if h >= 2:
                            dve.wait_ge(sem("dS_ps"), 2 + h - 1)
                        tell(V.tensor_tensor(vexp[h % 2][:, :, 0:DK], bc(B_VN[0:R, h, :], 1, NSEQ), bc(inds[:, :], 2, DK), ALU.mult), "vx")
                        link(V.tensor_tensor(S[:, :, h, :], S[:, :, h, :], bc(egx[:, :, h], 2, DK), ALU.mult))
                        dve.wait_ge(sem("dS_ps"), 2 + h + 1)
                        V.tensor_tensor(S[:, 0:4, h, :], S[:, 0:4, h, :], ps(2, P, P), ALU.add)
                        tell(V.tensor_tensor(S[:, 4:8, h, :], S[:, 4:8, h, :], ps(3, P, P), ALU.add), "Ss_done")

                def head_norm(src, scratch, out, i):
                    link(V.tensor_tensor(scratch[0:R, :, :], src, src, ALU.mult))
                    link(V.tensor_reduce(st[0:R, t, i, :], scratch[0:R, :, :], AX, ALU.add))
                    tell(V.tensor_scalar(st[0:R, t, i, :], st[0:R, t, i, :], 1.0 / DK, EPS, ALU.mult, ALU.add), "hms")
                    dve.wait_ge(sem("hrs"), 2 * t + i + 1)
                    return V.tensor_tensor(out[0:R, :, :], src, bc(ms[0:R, t, 10 + i, :], 2, DK), ALU.mult)

                tell(head_norm(B_O[0:R, :, :], B_ED, B_DG, 0), "on")
                dve.wait_ge(sem("mixT_ps"), 2 * t + 1)
                if t == 0:
                    dve.wait_ge(sem("szg"), 8)
                    dve.wait_ge(sem("proj"), len(PROD))
                tell(V.tensor_tensor(xT[:, 0:4, tk], ps(0, R, P), szo[:, 0:4, tk], ALU.mult), "mix")
                m = lambda i: ms[0:R, t, i, :]
                tell(V.tensor_tensor(M_DG[0:R, :, 0:R], bc(ident[0:R, 0:R], 1, H), bc(igc[0:R, t, :], 2, R), ALU.mult), "diag")
                if t == 1:
                    V.tensor_copy(m(MPREV), ms[:, 0, MNEW, :])
                if t == 2:
                    dve.wait_ge(sem("S_in"), 32 * NSEQ)
                dve.wait_ge(sem("C_ps"), t + 1)
                Cps = PB[4][0:R, 0:4 * R].rearrange("p (h x) -> p h x", h=H)
                link(V.tensor_tensor(M_P[0:R, :, 0:R], Cps, bc(nL, 1, H), ALU.add))
                link(V.tensor_reduce(m(MCUM), M_P[0:R, :, 0:R], AX, ALU.max))
                link(V.tensor_tensor(m(MCUM), m(MCUM), m(MPREV), ALU.max))
                tell(V.tensor_tensor(m(MT), gcb[0:R, t, 4:8], m(MCUM), ALU.add), "mt")
                V.tensor_tensor(M_P[0:R, :, 0:R], M_P[0:R, :, 0:R], bc(m(MCUM), 2, R), ALU.subtract)
                link(V.tensor_tensor(m(EINT), m(MPREV), m(MCUM), ALU.subtract))
                dve.wait_ge(sem("mt"), t + 1)
                tell(V.tensor_scalar(m(EMT), m(MT), -1.0, None, ALU.mult), "marg")
                dve.wait_ge(sem("pexp"), t + 1)
                dve.wait_ge(sem("qkb_ps"), t + 1)
                tell(V.tensor_tensor(M_S[0:R, :, 0:R], ps(5, R), M_P[0:R, :, 0:R], ALU.mult), "s")
                dve.wait_ge(sem("mnew_ps"), t + 1)
                ins = V.tensor_copy(m(MNEW), PB[7][0:R, 0:H])
                tell(ins, "mnew")
                dve.wait_ge(sem("mnew"), t + 1)
                V.tensor_tensor(m(WL), igc[0:R, t, :], m(MNEW), ALU.subtract)
                link(V.tensor_tensor(m(FT), m(MPREV), m(MNEW), ALU.subtract))
                tell(V.tensor_tensor(ms[0:R, t, WL:FT + 1, :], ms[0:R, t, WL:FT + 1, :], bc(gto[0:R, t, 4:8], 1, 2), ALU.add), "warg")
                dve.wait_ge(sem("sT_ps"), t + 1)
                tell(V.tensor_copy(M_ST[0:R, :, 0:R], ps(5, R)), "sT")
                link(V.memset(M_KW[0:R, :, :], 0.0))
                dve.wait_ge(sem("wexp"), t + 1)
                dve.wait_ge(sem("kb_ps"), t + 1)
                for hh in range(2):
                    ins = V.tensor_tensor(M_KW[0:R, hh::2, 64 * hh:64 * hh + 64],
                                          PB[6][0:R, 0:256].rearrange("p (q x) -> p q x", q=2)[:, :, 64 * hh:64 * hh + 64],
                                          bc(ms[0:R, t, WL, hh::2], 2, DQ), ALU.mult)
                tell(ins, "kw")
                dve.wait_ge(sem("mexp"), t + 1)
                if t == 2:
                    dve.wait_ge(sem("qCT_ps"), 1)
                    V.tensor_tensor(qnx[:, :, :], PB[3][0:R, 256:288].rearrange("p (h s) -> p h s", h=H), bc(inds[:, :], 1, H), ALU.mult)
                    link(V.tensor_copy(stage[:, 0:256], PB[3][:, 0:256]))
                    tell(V.tensor_tensor(fx[:, :, :], bc(ms[0:R, t, FT, :], 1, NSEQ), bc(lasts[:, :], 2, H), ALU.mult), "fx")
                    dve.wait_ge(sem("fx"), 1)
                    V.nop().then_inc(sem("qCT"), 1)
                    link(V.tensor_reduce(M_NUM[0:R, :, DK], qnx[:, :, :], AX, ALU.add))
                    link(V.tensor_tensor(M_NUM[0:R, :, DK], M_NUM[0:R, :, DK], m(EINT), ALU.mult))
                dve.wait_ge(sem("num_ps"), t + 1)
                if t == 1:
                    dve.wait_ge(sem("qC_ps"), 1)
                if t == 2:
                    dve.wait_ge(sem("qC_ps"), 2)
                    link(V.tensor_tensor(M_NUM[0:R, :, 0:DK], ps(4, P), bc(m(EINT), 2, DK), ALU.mult))
                for q in range(2):
                    dst = M_NUM[0:R, 2 * q:2 * q + 2, :]
                    src = PB[1 + q][0:R, 0:258].rearrange("p (h v) -> p h v", h=2)
                    if t == 0:
                        ins = V.tensor_copy(dst, src)
                    else:
                        if t == 1:
                            link(V.tensor_tensor(dst, PB[3 + q][0:R, 0:258].rearrange("p (h v) -> p h v", h=2),
                                                 bc(ms[0:R, t, EINT, 2 * q:2 * q + 2], 2, DK + 1), ALU.mult))
                        ins = V.tensor_tensor(dst, dst, src, ALU.add)
                    link(ins)
                link(V.scalar_tensor_tensor(m(DEN), M_NUM[0:R, :, DK], -1.0, M_NUM[0:R, :, DK], ALU.mult, ALU.max))
                link(V.tensor_tensor(m(DEN), m(DEN), m(EMT), ALU.max))
                link(V.reciprocal(m(RDEN), m(DEN)))
                link(V.tensor_tensor(B_WT[0:R, :, :], M_NUM[0:R, :, 0:DK], bc(m(RDEN), 2, DK), ALU.mult))
                if t == 0:
                    dve.wait_ge(sem("dC_ps"), 1)
                    tell(V.tensor_copy(Cp, PB[6][:, 0:258].rearrange("p (q v) -> p q v", q=2)), "Cp_done")
                elif t == 1:
                    V.tensor_copy(ftp[0:64, 0, :], ms[0:64, 1, FT, 0::2])
                    link(V.tensor_copy(ftp[64:128, 0, :], ms[64:128, 1, FT, 1::2]))
                    link(V.tensor_tensor(Cp, Cp, bc(ftp[:, 0, :], 2, DK + 1), ALU.mult))
                    dve.wait_ge(sem("dC_ps"), 2)
                    tell(V.tensor_tensor(Cp, Cp, PB[6][:, 0:258].rearrange("p (q v) -> p q v", q=2), ALU.add), "Cp_done")
                else:
                    dve.wait_ge(sem("ft_ps"), 1)
                    for hh in range(2):
                        ins = V.tensor_copy(ftp[64 * hh:64 * hh + 64, :, :],
                                            PB[7][64 * hh:64 * hh + 64, 0:NSEQ * H].rearrange("p (s h) -> p s h", h=H)[:, :, hh::2])
                    link(ins)
                    for q in range(2):
                        if q > 0:
                            dve.wait_ge(sem("dC_ps"), 3)
                        for hh in range(2):
                            ins = V.tensor_tensor(vexp[hh][:, :, :], bc(va[0:R, 2, 2 * q + hh, :], 1, NSEQ), bc(inds[:, :], 2, DK + 1), ALU.mult)
                        tell(ins, "vx")
                        link(V.tensor_tensor(Cs[:, :, q, :], Cs[:, :, q, :], bc(ftp[:, :, q], 2, DK + 1), ALU.mult))
                        dve.wait_ge(sem("dC_ps"), 3 + q)
                        for nn, (s0, s1) in enumerate([(0, 3), (3, 6), (6, 8)]):
                            ins = V.tensor_tensor(Cs[:, s0:s1, q, :], Cs[:, s0:s1, q, :],
                                                  PB[[5, 6, 0][nn]][:, 0:129 * (s1 - s0)].rearrange("p (s v) -> p s v", v=129), ALU.add)
                        tell(ins, "Cs_done")
                tell(head_norm(B_WT[0:R, :, :], B_ED, B_O, 1), "hn")
                dve.wait_ge(sem("mixT_ps"), 2 * t + 2)
                tell(V.tensor_tensor(xT[:, 4:8, tk], ps(3, R, P), szo[:, 4:8, tk], ALU.mult), "mix")
            V.nop().then_inc(sem("xs_free"), 1)
            for i in range(6):
                t, m2 = i // 2, i % 2
                R = ROWS[t]
                dve.wait_ge(sem("x1_ps"), i + 1)
                dst = X[0:R, t, 512 * m2:512 * m2 + 512]
                tell(V.tensor_tensor(dst, dst, PB[i % 4][0:R, :], ALU.add), "x1")
            norm(1)
            xT_out(1, 8, 4)
            dve.wait_ge(sem("lg_ps"), 1)
            dve.wait_ge(sem("rw_in"), 32)
            V.tensor_tensor(lg[:, 0:2, :], PB[0][:, 0:64].rearrange("p (t e) -> p t e", t=2), bc(rbias[:, :], 1, 2), ALU.add)
            link(V.tensor_tensor(lg[0:64, 2, :], PB[0][0:64, 64:96], rbias[0:64, :], ALU.add))
            top = scf[:, 7424:7424 + 24].rearrange("p (t x) -> p t x", t=3)
            for t in range(3):
                ins = V.max(top[:, t, :], lg[:, t, :])
            link(ins)
            M_, E_, GT, EQ, INC, W1 = t3[0], t3[1], t3[2], t3[3], t3[4], t3[5]
            c4 = scf[:, 7460:7463]
            c5 = scf[:, 7464:7467]
            V.tensor_tensor(GT, lg[:], bc(top[:, :, 3], 2, NE), ALU.is_gt)
            V.tensor_tensor(EQ, lg[:], bc(top[:, :, 3], 2, NE), ALU.is_equal)
            tell(V.tensor_tensor(E_, lg[:], bc(top[:, :, 0], 2, NE), ALU.subtract), "larg")
            dve.wait_ge(sem("larg"), 1)
            for t in range(3):
                ins = V.tensor_tensor_scan(INC[:, t, :], ones[:, 0:NE], EQ[:, t, :], 0.0, ALU.mult, ALU.add)
            link(V.tensor_reduce(c4, GT, AX, ALU.add))
            link(V.tensor_scalar(c4, c4, -1.0, float(TOPK), ALU.mult, ALU.add))
            link(V.tensor_tensor(INC, INC, bc(c4, 2, NE), ALU.is_le))
            link(V.tensor_tensor(EQ, EQ, INC, ALU.mult))
            tell(V.tensor_tensor(M_, GT, EQ, ALU.add), "member")
            dve.wait_ge(sem("member"), 1)
            dve.wait_ge(sem("lexp"), 1)
            link(V.tensor_tensor(E_, E_, M_, ALU.mult))
            link(V.tensor_reduce(c5, E_, AX, ALU.add))
            link(V.reciprocal(c5, c5))
            tell(V.tensor_tensor(gateb[:, :, 0:NE], E_, bc(c5, 2, NE), ALU.mult), "gates")
            dve.wait_ge(sem("gates"), 1)
            dve.wait_ge(sem("pos_ps"), 1)
            link(V.scalar_tensor_tensor(posb[:, 0:2, 0:NE], PB[1][:, 0:64].rearrange("p (t e) -> p t e", t=2), 1.0, M_[:, 0:2, :],
                                        ALU.add, ALU.mult))
            link(V.scalar_tensor_tensor(posb[0:64, 2, 0:NE], PB[1][0:64, 64:96], 1.0, M_[0:64, 2, :], ALU.add, ALU.mult))
            link(V.memset(posb[64:128, 2, 0:NE], 0.0))
            link(V.tensor_scalar(posb[:, :, 0:NE], posb[:, :, 0:NE], -1.0, None, ALU.add))
            cnt, nov, cum, first = t1[0], t1[1], t1[2], t1[3]
            link(V.tensor_copy(cnt, PB[1][:, 96:96 + NE]))
            link(V.tensor_scalar(nov, cnt, float(SL), None, ALU.is_gt))
            for k in range(2, -(-NTOK // SL)):
                link(V.scalar_tensor_tensor(nov, cnt, float(SL * k), nov, ALU.is_gt, ALU.add))
            link(V.tensor_tensor_scan(cum, ones[:, 0:NE], nov, 0.0, ALU.mult, ALU.add))
            link(V.tensor_tensor(first, cum, nov, ALU.subtract))
            V.tensor_scalar(ntotf[:, 0:1], cum[:, NE - 1:NE], float(NE), None, ALU.add)
            link(V.tensor_scalar(ntotf[:, 1:2], cum[:, NE - 1:NE], float(NE - 1), None, ALU.add))
            V.tensor_copy(ntot[:], ntotf[:])
            ej, fj, sj = scf[:, 7480:7480 + NOV], scf[:, 7510:7510 + NOV], scf[:, 7540:7540 + NOV]
            link(V.tensor_tensor(tb[0], bc(iota_s[:, 0:NOV], 2, NE), bc(cum, 1, NOV), ALU.is_ge))
            link(V.tensor_reduce(ej, tb[0], AX, ALU.add))
            link(V.tensor_tensor(tb[0], bc(iota_s[:, 0:NE], 1, NOV), bc(ej, 2, NE), ALU.is_equal))
            link(V.tensor_tensor(tb[1], tb[0], bc(first, 1, NOV), ALU.mult))
            link(V.tensor_reduce(fj, tb[1], AX, ALU.add))
            link(V.tensor_tensor(sj, iota_s[:, 0:NOV], fj, ALU.subtract))
            link(V.tensor_scalar(sj, sj, float(SL), float(SL), ALU.mult, ALU.add))
            for t in range(3):
                for src, dst in ((posb, posb), (gateb, gateb)):
                    link(V.tensor_tensor(tb[1], tb[0], bc(src[:, t, 0:NE], 1, NOV), ALU.mult))
                    link(V.tensor_reduce(dst[:, t, NE:NB], tb[1], AX, ALU.add))
                link(V.tensor_tensor(posb[:, t, NE:NB], posb[:, t, NE:NB], sj, ALU.subtract))
            V.tensor_copy(etabf[:, 0:NE], iota_s[:, 0:NE])
            link(V.tensor_scalar(etabf[:, NE:NB], ej, float(NE - 1), None, ALU.min))
            tell(V.tensor_copy(etab[:], etabf[:]), "tables")
            dve.wait_ge(sem("tables"), 1)

            for i in range(6):
                t, m2 = i // 2, i % 2
                R = ROWS[t]
                dve.wait_ge(sem("x1_ps"), 6 + i + 1)
                dst = X[0:R, t, 512 * m2:512 * m2 + 512]
                V.tensor_tensor(dst, dst, PB[4 + m2][0:R, :], ALU.add).then_inc(sem("x1"), 1)
            dve.wait_ge(sem("x1"), 12)

            def select(b):
                for t in range(3):
                    ins = V.tensor_scalar(SEL_r[:, t, :], iota_s[:], posb[:, t, bass.ds(b, 1)], None, ALU.is_equal)
                tell(ins, "sel")

            def select_gated(b):
                for t in range(3):
                    ins = V.tensor_scalar(SELG[:, t, :, :], bc(iota_s[:], 1, 2), posb[:, t, bass.ds(b, 1)], gateb[:, t, bass.ds(b, 1)],
                                          ALU.is_equal, ALU.mult)
                tell(ins, "selg")

            def low(b, c):
                if c not in POOL_LO:
                    dve.wait_ge(sem("hi"), NCK * b + c + 1)
                    V.tensor_tensor(raw_r(c), raw(c), hi_r(c), ALU.subtract).then_inc(sem("lo_dve"), 1)

            def add_y(b, i):
                t, m2 = i // 2, i % 2
                R = ROWS[t]
                dve.wait_ge(sem("x2_ps"), 6 * b + i + 1)
                dst = X[0:R, t, 512 * m2:512 * m2 + 512]
                V.tensor_tensor(dst, dst, PB[4 + m2][0:R, :], ALU.add).then_inc(sem("x2"), 1)

            def expert(b, first):
                e = dve.value_load(etab[0:1, bass.ds(b, 1)], min_val=0, max_val=NE - 1)
                low(b, 0)
                low(b, 1)
                select(b + 1)
                for c in range(2, NGU):
                    low(b, c)
                    if c >= 4 and not first:
                        add_y(b - 1, c - 4)
                select_gated(b)
                dve.wait_ge(sem("w_used"), NCK * b + NGU)
                V.tensor_copy(hS[:, 1024:1536], PB[2][:, :])
                V.tensor_copy(hS[:, 1536:2048], PB[3][:, :]).then_inc(sem("hS"), 1)
                if not first:
                    add_y(b - 1, 4)
                    add_y(b - 1, 5)

                def half_bank(b0, i, h):
                    return PB[b0 + i][:, :].rearrange("p (k h s) -> p k h s", k=4, h=2)[:, :, h, :]

                def biased(out, b0, c0):
                    for i in range(2):
                        ins = V.tensor_tensor(out[:, 4 * i:4 * i + 4, :], half_bank(b0, i, 0),
                                              bgu[:, c0 + 4 * i:c0 + 4 * i + 4, bass.ds(e, 1)].to_broadcast([P, 4, SL]), ALU.add)
                    ins.then_inc(sem("lp"), 1)

                def plus_rest(out, b0):
                    for i in range(2):
                        o4 = out[:, 4 * i:4 * i + 4, :]
                        ins = V.tensor_tensor(o4, o4, half_bank(b0, i, 1), ALU.add)
                    ins.then_inc(sem("lp"), 1)

                dve.wait_ge(sem("hT_ps"), 2 * b + 1)
                biased(gt, 0, 0)
                dve.wait_ge(sem("lp"), 8 * b + 1)
                plus_rest(gt, 0)
                dve.wait_ge(sem("lp"), 8 * b + 2)
                V.tensor_scalar(gt, gt, LIMIT, None, ALU.min).then_inc(sem("gt"), 1)
                dve.wait_ge(sem("hT_ps"), 2 * b + 2)
                biased(ut, 2, 8)
                dve.wait_ge(sem("lp"), 8 * b + 3)
                plus_rest(ut, 2)
                dve.wait_ge(sem("lp"), 8 * b + 4)
                V.tensor_scalar(ut, ut, LIMIT, -LIMIT, ALU.min, ALU.max).then_inc(sem("lp"), 1)
                dve.wait_ge(sem("lp"), 8 * b + 5)
                dve.wait_ge(sem("gt"), b + 1)
                V.scalar_tensor_tensor(ut, ut, 1.0, gt, ALU.add, ALU.mult).then_inc(sem("lp"), 1)
                dve.wait_ge(sem("lp"), 8 * b + 6)
                dve.wait_ge(sem("sig"), b + 1)
                V.tensor_tensor(act_t, ut, sg, ALU.mult).then_inc(sem("lp"), 1)
                dve.wait_ge(sem("lp"), 8 * b + 7)
                V.tensor_copy(ag_r[:, :, 0, :], act_t).then_inc(sem("lp"), 1)
                dve.wait_ge(sem("lp"), 8 * b + 8)
                V.tensor_tensor(ag_r[:, :, 1, :], act_t, ag_r[:, :, 0, :], ALU.subtract).then_inc(sem("act"), 1)
                for c in range(9, NCK):
                    low(b, c)

            total = dve.value_load(ntot[0:1, 0:1], min_val=NE, max_val=NB - 1)
            select(0)
            expert(0, True)
            with dve.Fori(1, total) as b:
                expert(b, False)
            last_b = dve.value_load(ntot[0:1, 1:2], min_val=NE - 1, max_val=NB - 2)
            for i in range(6):
                add_y(last_b, i)
            norm(2)
            xT_out(2, 16, 4)
            for i in range(6):
                t, m2 = i // 2, i % 2
                R = ROWS[t]
                dve.wait_ge(sem("gate"), i + 1)
                dve.wait_ge(sem("pw"), i + 1)
                link(V.tensor_tensor(gsc[i % 2][0:R, :], gsc[i % 2][0:R, :], pw[0:R, t, 512 * m2:512 * m2 + 512], ALU.mult))
                dst = X[0:R, t, 512 * m2:512 * m2 + 512]
                tell(V.tensor_tensor(dst, dst, gsc[i % 2][0:R, :], ALU.add), "x3")
                if m2 == 1:
                    dve.wait_ge(sem("ss"), 9 + t + 1)
                    tell(V.tensor_scalar(nst[0:R, 1, t:t + 1], nst[0:R, 0, t:t + 1], 1.0 / D, EPS, ALU.mult, ALU.add), "ms")
                    dve.wait_ge(sem("rs"), 3 + t + 1)
                    dve.wait_ge(sem("last_in"), 32)
                    tell(V.scalar_tensor_tensor(X[0:R, t, :], X[0:R, t, :], nst[0:R, 2, t:t + 1], fgain[0:R, :],
                                                ALU.mult, ALU.mult), "y_ready")


_INS = ["x_prompt", "x_sample", "p_prompt", "p_sample", "state_conv", "state_gdn", "state_mlstm_c", "state_mlstm_n",
        "state_mlstm_m", "norm_attn_g", "w_in", "conv_w", "gdn_a_log", "gdn_dt_bias", "gdn_norm_g", "mlstm_i_bias",
        "mlstm_f_bias", "mlstm_norm_g", "w_out", "norm_moe_g", "router_w", "router_b", "expert_w_gu", "expert_b_gu",
        "expert_w_down", "expert_b_down", "norm_ple_g", "ple_gate_w", "ple_w", "final_norm_g"]
_OUTS = [("y_p", (1, TP, D)), ("y_s", (NSEQ, LS, D)), ("conv_p", (1, 1, CW - 1, NCH * P)), ("gdn_p", (1, 1, H, DK, DK)),
         ("c_p", (1, 1, H, DQ, DK)), ("n_p", (1, 1, H, DQ)), ("m_p", (1, 1, H)),
         ("conv_s", (1, NSEQ, CW - 1, NCH * P)), ("gdn_s", (1, NSEQ, H, DK, DK)), ("c_s", (1, NSEQ, H, DQ, DK)),
         ("n_s", (1, NSEQ, H, DQ)), ("m_s", (1, NSEQ, H))]


def kernel(**inputs):
    import numpy as _np
    import concourse.bacc as _bacc
    from concourse import mybir as _mybir
    from concourse.bass_utils import run_bass_kernel_spmd as _run

    nc = _bacc.Bacc("TRN2", target_bir_lowering=False, num_devices=1)
    arrays, a, o = {}, {}, {}
    for name in _INS:
        v = _np.ascontiguousarray(inputs[name])
        arrays[f"in_{name}"] = v
        a[name] = nc.dram_tensor(f"in_{name}", v.shape, _mybir.dt.from_np(v.dtype), kind="ExternalInput").ap()
    for name, shape in _OUTS:
        o[name] = nc.dram_tensor(f"out_{name}", shape, _mybir.dt.float32, kind="ExternalOutput").ap()
    build(nc, a, o)
    r = _run(nc, [arrays], core_ids=[0])
    return tuple(r.results[0][f"out_{name}"] for name, _ in _OUTS)
```
